# Optimizing a Trainium2 kernel written in Bass

```python
import math
import jax, jax.numpy as jnp
from jax import lax
import numpy as np

D_MODEL = 1024
BATCH = 1
SEQ = 1024
DEPTH = 2

GRID_W = 64
CTX_LEN = 256

SSD_EXPAND = 2
SSD_DI = SSD_EXPAND * D_MODEL
SSD_HEADDIM = 64
SSD_HEADS = SSD_DI // SSD_HEADDIM
SSD_STATE = 128
SSD_GROUPS = 8
SSD_CONV = 3
SSD_CHUNK = 128
SSD_CONV_CH = SSD_DI + 2 * SSD_GROUPS * SSD_STATE
SSD_IN = SSD_DI + SSD_CONV_CH + 2 * SSD_HEADS

NA_HEADS = 16
NA_HEADDIM = 64
NA_DI = NA_HEADS * NA_HEADDIM
WIN_R = 8
WIN_C = 16

N_SSD_LAYERS = (DEPTH + 1) // 2
N_NA_LAYERS = DEPTH // 2
RMS_EPS = 1e-6

kernel_name = "hybrid_ssd_natten_prefix_dit"

def _rms(x, g):
    xf = x.astype(jnp.float32)
    y = xf * lax.rsqrt(jnp.mean(xf * xf, axis=-1, keepdims=True) + RMS_EPS)
    return (y * g.astype(jnp.float32)).astype(x.dtype)

def _dwconv(u, w, b):
    k, ch = w.shape
    out = lax.conv_general_dilated(u, w[:, None, :].astype(u.dtype), window_strides=(1,),
                                   padding=[(k // 2, k // 2)],
                                   dimension_numbers=('NWC', 'WIO', 'NWC'),
                                   feature_group_count=ch)
    return out + b.astype(u.dtype)

def _ssd_scan(x, dt, A, Bm, Cm, h0):
    b, l, H, P = x.shape
    G, N = Bm.shape[-2:]
    K = H // G
    L = SSD_CHUNK
    nc = l // L
    f32 = jnp.float32
    xc = x.astype(f32).reshape(b, nc, L, G, K, P)
    dtc = dt.astype(f32).reshape(b, nc, L, G, K)
    a = dtc * A.astype(f32).reshape(G, K)
    Bc = Bm.astype(f32).reshape(b, nc, L, G, N)
    Cc = Cm.astype(f32).reshape(b, nc, L, G, N)
    a_cum = jnp.cumsum(a, axis=2)
    seg = a_cum[:, :, :, None] - a_cum[:, :, None, :]
    tri = jnp.tril(jnp.ones((L, L), dtype=bool))[None, None, :, :, None, None]
    decay = jnp.exp(jnp.where(tri, seg, -jnp.inf))
    cb = jnp.einsum('bclgn,bcsgn->bclsg', Cc, Bc)
    xdt = xc * dtc[..., None]
    y_diag = jnp.einsum('bclsgk,bcsgkp->bclgkp', cb[..., None] * decay, xdt)
    decay_out = jnp.exp(a_cum[:, :, -1:] - a_cum)
    states = jnp.einsum('bclgn,bclgk,bclgkp->bcgkpn', Bc, decay_out, xdt)
    chunk_decay = jnp.exp(a_cum[:, :, -1])

    def step(h, inp):
        s, d = inp
        return h * d[..., None, None] + s, h

    hT, h_prev = lax.scan(step, h0.astype(f32).reshape(b, G, K, P, N),
                          (jnp.moveaxis(states, 1, 0), jnp.moveaxis(chunk_decay, 1, 0)))
    h_prev = jnp.moveaxis(h_prev, 0, 1)
    y_off = jnp.einsum('bclgn,bcgkpn,bclgk->bclgkp', Cc, h_prev, jnp.exp(a_cum))
    y = (y_diag + y_off).reshape(b, l, H, P)
    return y, hT.reshape(b, H, P, N)

def _ssd_scan_rev(x, dt, A, Bm, Cm, h0):
    y, hT = _ssd_scan(jnp.flip(x, 1), jnp.flip(dt, 1), A, jnp.flip(Bm, 1), jnp.flip(Cm, 1), h0)
    return jnp.flip(y, 1), hT

def _ssd_mixer(h_l, h_c, w_in, conv_w, conv_b, dt_bias, a_log, d_skip, norm_g, w_out, ctx_out):
    GN = SSD_GROUPS * SSD_STATE

    def proj(h):
        b, n, _ = h.shape
        t = h @ w_in
        z = t[..., :SSD_DI]
        xbc = jax.nn.silu(_dwconv(t[..., SSD_DI:SSD_DI + SSD_CONV_CH], conv_w, conv_b))
        xs = xbc[..., :SSD_DI].reshape(b, n, SSD_HEADS, SSD_HEADDIM)
        Bm = xbc[..., SSD_DI:SSD_DI + GN].reshape(b, n, SSD_GROUPS, SSD_STATE)
        Cm = xbc[..., SSD_DI + GN:].reshape(b, n, SSD_GROUPS, SSD_STATE)
        dt = t[..., SSD_DI + SSD_CONV_CH:].astype(jnp.float32).reshape(b, n, 2, SSD_HEADS)
        dt = jax.nn.softplus(dt + dt_bias.astype(jnp.float32))
        return z, xs, Bm, Cm, dt

    def finish(y, xs, z):
        b, n = xs.shape[:2]
        y = y + xs.astype(jnp.float32) * d_skip.astype(jnp.float32)[:, None]
        y = (y.reshape(b, n, SSD_DI) * jax.nn.silu(z.astype(jnp.float32)))
        y = y.reshape(b, n, SSD_GROUPS, SSD_DI // SSD_GROUPS)
        y = y * lax.rsqrt(jnp.mean(y * y, axis=-1, keepdims=True) + RMS_EPS)
        y = (y.reshape(b, n, SSD_DI) * norm_g.astype(jnp.float32)).astype(xs.dtype)
        return y @ w_out

    A = -jnp.exp(a_log.astype(jnp.float32))
    zc, xc, Bc, Cc, dtc = proj(h_c)
    zl, xl, Bl, Cl, dtl = proj(h_l)
    h0 = jnp.zeros((h_l.shape[0], SSD_HEADS, SSD_HEADDIM, SSD_STATE), jnp.float32)
    yc_f, s_f = _ssd_scan(xc, dtc[:, :, 0], A[0], Bc, Cc, h0)
    yc_b, s_b = _ssd_scan_rev(xc, dtc[:, :, 1], A[1], Bc, Cc, h0)
    yl_f, _ = _ssd_scan(xl, dtl[:, :, 0], A[0], Bl, Cl, s_f)
    yl_b, _ = _ssd_scan_rev(xl, dtl[:, :, 1], A[1], Bl, Cl, s_b)
    out_l = finish(yl_f + yl_b, xl, zl)
    out_c = finish(yc_f + yc_b, xc, zc) if ctx_out else None
    return out_l, out_c

def _na_mixer(h_l, h_c, w_in, rpb, w_out, ctx_out):
    b, n, _ = h_l.shape
    rows = n // GRID_W
    kr = min(WIN_R, rows)
    scale = NA_HEADDIM ** -0.5
    tl = (h_l @ w_in).reshape(b, n, 4, NA_HEADS, NA_HEADDIM)
    tc = (h_c @ w_in).reshape(b, h_c.shape[1], 4, NA_HEADS, NA_HEADDIM)
    q_l, k_l, v_l, g_l = tl[:, :, 0], tl[:, :, 1], tl[:, :, 2], tl[:, :, 3]
    q_c, k_c, v_c, g_c = tc[:, :, 0], tc[:, :, 1], tc[:, :, 2], tc[:, :, 3]

    grid = (b, rows, GRID_W, NA_HEADS, NA_HEADDIM)
    qg, kgrid, vgrid = q_l.reshape(grid), k_l.reshape(grid), v_l.reshape(grid)
    r_idx = jnp.arange(rows)
    row_start = jnp.clip(r_idx - kr // 2, 0, rows - kr)
    row_sel = row_start[:, None] + jnp.arange(kr)[None, :]
    kg = kgrid[:, row_sel]
    vg = vgrid[:, row_sel]

    cols = jnp.arange(GRID_W)
    col_start = jnp.clip(cols - WIN_C // 2, 0, GRID_W - WIN_C)
    col_mask = (cols[None, :] >= col_start[:, None]) & (cols[None, :] < col_start[:, None] + WIN_C)
    roff = row_sel - r_idx[:, None] + (WIN_R - 1)
    coff = jnp.clip(cols[None, :] - cols[:, None], -(WIN_C - 1), WIN_C - 1) + (WIN_C - 1)
    bias = rpb.astype(jnp.float32)[:, roff[:, None, :, None], coff[None, :, None, :]]

    s_win = jnp.einsum('brqhd,brkwhd->bhrqkw', qg, kg).astype(jnp.float32) * scale + bias[None]
    s_win = jnp.where(col_mask[None, None, None, :, None, :], s_win, -jnp.inf)
    s_ctx = jnp.einsum('brqhd,bchd->bhrqc', qg, k_c).astype(jnp.float32) * scale
    s = jnp.concatenate([s_win.reshape(b, NA_HEADS, rows, GRID_W, kr * GRID_W), s_ctx], axis=-1)
    p = jax.nn.softmax(s, axis=-1).astype(v_l.dtype)
    p_win = p[..., :kr * GRID_W].reshape(b, NA_HEADS, rows, GRID_W, kr, GRID_W)
    p_ctx = p[..., kr * GRID_W:]
    o = jnp.einsum('bhrqkw,brkwhd->brqhd', p_win, vg) + jnp.einsum('bhrqc,bchd->brqhd', p_ctx, v_c)
    out_l = (o.reshape(b, n, NA_DI) * jax.nn.silu(g_l.reshape(b, n, NA_DI))) @ w_out

    out_c = None
    if ctx_out:
        sc = jnp.einsum('bqhd,bkhd->bhqk', q_c, k_c).astype(jnp.float32) * scale
        pc = jax.nn.softmax(sc, axis=-1).astype(v_c.dtype)
        oc = jnp.einsum('bhqk,bkhd->bqhd', pc, v_c).reshape(b, -1, NA_DI)
        out_c = (oc * jax.nn.silu(g_c.reshape(b, -1, NA_DI))) @ w_out
    return out_l, out_c

def setup_inputs(seed: int = 0) -> dict:
    key = jax.random.key(seed)
    ks = jax.random.split(key, 24)
    D = D_MODEL
    nrm = jax.random.normal
    x = nrm(ks[0], (BATCH, SEQ, D), jnp.float32)
    c = nrm(ks[1], (BATCH, D), jnp.float32)
    ctx = nrm(ks[2], (BATCH, CTX_LEN, D), jnp.float32)
    c_ctx = nrm(ks[3], (D,), jnp.float32)
    ada_w = nrm(ks[4], (DEPTH, D, 3 * D), jnp.float32) * D ** -0.5
    ada_b = nrm(ks[5], (DEPTH, 3 * D), jnp.float32) * 0.02
    pre_g = 1.0 + 0.02 * nrm(ks[6], (DEPTH, D), jnp.float32)
    post_g = 1.0 + 0.02 * nrm(ks[7], (DEPTH, D), jnp.float32)
    ssd_w_in = nrm(ks[8], (N_SSD_LAYERS, D, SSD_IN), jnp.float32) * D ** -0.5
    ssd_conv_w = nrm(ks[9], (N_SSD_LAYERS, SSD_CONV, SSD_CONV_CH), jnp.float32) * SSD_CONV ** -0.5
    ssd_conv_b = nrm(ks[10], (N_SSD_LAYERS, SSD_CONV_CH), jnp.float32) * 0.02
    u = jax.random.uniform(ks[11], (N_SSD_LAYERS, 2, SSD_HEADS), jnp.float32)
    dt0 = jnp.exp(u * (math.log(0.1) - math.log(0.001)) + math.log(0.001))
    ssd_dt_bias = dt0 + jnp.log(-jnp.expm1(-dt0))
    ssd_a_log = jnp.log(jax.random.uniform(ks[12], (N_SSD_LAYERS, 2, SSD_HEADS), jnp.float32, 1.0, 16.0))
    ssd_d = 1.0 + 0.1 * nrm(ks[13], (N_SSD_LAYERS, SSD_HEADS), jnp.float32)
    ssd_norm_g = 1.0 + 0.02 * nrm(ks[14], (N_SSD_LAYERS, SSD_DI), jnp.float32)
    ssd_w_out = nrm(ks[15], (N_SSD_LAYERS, SSD_DI, D), jnp.float32) * SSD_DI ** -0.5
    na_w_in = nrm(ks[16], (N_NA_LAYERS, D, 4 * NA_DI), jnp.float32) * D ** -0.5
    na_rpb = nrm(ks[17], (N_NA_LAYERS, NA_HEADS, 2 * WIN_R - 1, 2 * WIN_C - 1), jnp.float32) * 0.1
    na_w_out = nrm(ks[18], (N_NA_LAYERS, NA_DI, D), jnp.float32) * NA_DI ** -0.5
    return {"x": x, "c": c, "ctx": ctx, "c_ctx": c_ctx,
            "ada_w": ada_w, "ada_b": ada_b, "pre_g": pre_g, "post_g": post_g,
            "ssd_w_in": ssd_w_in, "ssd_conv_w": ssd_conv_w, "ssd_conv_b": ssd_conv_b,
            "ssd_dt_bias": ssd_dt_bias, "ssd_a_log": ssd_a_log, "ssd_d": ssd_d,
            "ssd_norm_g": ssd_norm_g, "ssd_w_out": ssd_w_out,
            "na_w_in": na_w_in, "na_rpb": na_rpb, "na_w_out": na_w_out}

def reference(x, c, ctx, c_ctx, ada_w, ada_b, pre_g, post_g,
              ssd_w_in, ssd_conv_w, ssd_conv_b, ssd_dt_bias, ssd_a_log, ssd_d,
              ssd_norm_g, ssd_w_out, na_w_in, na_rpb, na_w_out):
    D = D_MODEL
    sc_l = jax.nn.silu(c)
    sc_c = jax.nn.silu(c_ctx)
    for i in range(DEPTH):
        last = i == DEPTH - 1
        mod_l = sc_l @ ada_w[i] + ada_b[i]
        mod_c = sc_c @ ada_w[i] + ada_b[i]
        shift_l, scale_l, gate_l = (mod_l[:, None, :D], mod_l[:, None, D:2 * D], mod_l[:, None, 2 * D:])
        shift_c, scale_c, gate_c = mod_c[:D], mod_c[D:2 * D], mod_c[2 * D:]
        h_l = _rms(x, pre_g[i]) * (1.0 + scale_l) + shift_l
        h_c = _rms(ctx, pre_g[i]) * (1.0 + scale_c) + shift_c
        j = i // 2
        if i % 2 == 0:
            out_l, out_c = _ssd_mixer(h_l, h_c, ssd_w_in[j], ssd_conv_w[j], ssd_conv_b[j],
                                      ssd_dt_bias[j], ssd_a_log[j], ssd_d[j], ssd_norm_g[j],
                                      ssd_w_out[j], not last)
        else:
            out_l, out_c = _na_mixer(h_l, h_c, na_w_in[j], na_rpb[j], na_w_out[j], not last)
        x = x + gate_l * _rms(out_l, post_g[i])
        if not last:
            ctx = ctx + gate_c * _rms(out_c, post_g[i])
    return x


_drawn_inputs = setup_inputs


def setup_inputs(seed=0):
    import zlib

    import numpy as np

    out = dict(_drawn_inputs(seed))
    spreads = {}
    factors = {'pre_g': 3.055,
     'post_g': 3.922,
     'ssd_conv_b': 4.705,
     'ssd_d': 27.44,
     'ssd_norm_g': 4.904,
     'na_rpb': 6.271}
    for name, (base, spread) in spreads.items():
        noise = np.random.default_rng([zlib.crc32(name.encode()), seed]).standard_normal(out[name].shape)
        drawn = base * np.exp(spread * noise) if base else spread * noise
        out[name] = __import__('jax').numpy.asarray(drawn.astype(out[name].dtype))
    for name, factor in factors.items():
        out[name] = (out[name] * factor).astype(out[name].dtype)
    return out
```

```python
from contextlib import ExitStack

import concourse.bass as bass
import numpy as np
from concourse import mybir

F32 = mybir.dt.float32
F32R = mybir.dt.float32r
ACT = mybir.ActivationFunctionType
ALU = mybir.AluOpType
AX_X = mybir.AxisListType.X

P = 128
D = 1024
KT = D // P
SEQ, CTX = 1024, 256
TOK = SEQ + CTX
NCH = TOK // P
CCH = CTX // P
DEPTH = 2
GROUPS, HPG, HD, NST = 8, 4, 64, 128
HEADS = GROUPS * HPG
DI = HEADS * HD
YT = DI // P
EPS = 1e-6
BLOCKS = ((0, 256), (256, 512), (768, 512))
NBL = len(BLOCKS)

UW = TOK + 4
TABS = 6
A_HI, A_LO, DT, DTDEC, ECUM, ETOT = range(TABS)


def ucol(t):
    return t + 1 if t < CTX else t + 3


class Mem:

    def __init__(self, nc, ctx, tag):
        self.nc, self.ctx, self.tag, self.sems = nc, ctx, tag, []
        ctx.callback(self.release)

    def release(self):
        if self.sems:
            self.nc.clear_and_free_semaphores(self.sems)
            self.nc.all_engine_barrier()

    def sb(self, name, shape, dt=F32):
        return self.ctx.enter_context(self.nc.sbuf_tensor(f"{self.tag}_{name}", shape, dt))

    def ps(self, name, dt=F32, n=512):
        return self.ctx.enter_context(self.nc.psum_tensor(f"{self.tag}_{name}", [P, n], dt))

    def sem(self, name):
        self.sems.append(self.nc.alloc_semaphore(f"{self.tag}_{name}"))
        return self.sems[-1]


def modulation(nc, a, mod_rows, mod_cols):
    NC = 512
    CH = 3 * D // NC
    RING = 4
    with ExitStack() as ctx:
        m = Mem(nc, ctx, "md")
        craw = m.sb("craw", [P, KT, 2])
        cth = m.sb("cth", [P, KT, 2])
        csil = m.sb("csil", [P, KT, 2])
        w = m.sb("w", [P, RING, KT, NC])
        brow = m.sb("brow", [2, DEPTH, 3 * D])
        rows = m.sb("rows", [2, DEPTH, 3 * D])
        ident = m.sb("ident", [2, 2])
        cols = m.sb("cols", [P, DEPTH, 2 * KT, 2])
        pacc = [m.ps(f"pacc{i}") for i in range(2)]
        pcol = m.ps("pcol")
        small, sil, acc, evac, colt, cole, stored = map(
            m.sem, ("small", "sil", "acc", "evac", "colt", "cole", "stored"))
        wld = [m.sem(f"wld{i}") for i in range(RING)]
        block = ctx.enter_context(nc.Block())
        N = DEPTH * CH

        @block.sync
        def _(sp):
            sp.dma_start(craw[:, :, :], a["cvec"]).then_inc(small, 16)
            sp.dma_start(ident[:, :], a["ident"][0:2, 0:2]).then_inc(small, 16)
            sp.dma_start(brow[:, :, :], a["ada_b"].partition_broadcast(2)).then_inc(small, 16)
            for n in range(N):
                i, c = divmod(n, CH)
                if n >= RING:
                    sp.wait_ge(acc, n - RING + 1)
                sp.dma_start(w[:, n % RING, :, :],
                             a["ada_w"][i].rearrange("(k p) n -> p k n", p=P)[:, :, c * NC:(c + 1) * NC]
                             ).then_inc(wld[n % RING], 16)
            sp.wait_ge(evac, N)
            sp.dma_start(mod_rows, rows[:, :, :]).then_inc(stored, 16)
            sp.wait_ge(cole, DEPTH)
            sp.dma_start(mod_cols, cols[:, :, :, :]).then_inc(stored, 16)
            sp.wait_ge(stored, 32)

        @block.scalar
        def _(act):
            act.wait_ge(small, 48)
            act.activation(cth[:, :, :], craw[:, :, :], ACT.Tanh, scale=0.5).then_inc(sil, 1)

        @block.vector
        def _(dve):
            dve.wait_ge(sil, 1)
            dve.scalar_tensor_tensor(csil[:, :, :], cth[:, :, :], 1.0, craw[:, :, :],
                                     ALU.add, ALU.mult).then_inc(sil, 1)
            dve.wait_ge(sil, 2)
            dve.tensor_scalar(csil[:, :, :], csil[:, :, :], 0.5, None, ALU.mult).then_inc(sil, 1)
            for n in range(N):
                i, c = divmod(n, CH)
                dve.wait_ge(acc, n + 1)
                dve.tensor_tensor(rows[:, i, c * NC:(c + 1) * NC], pacc[n % 2][0:2, :],
                                  brow[:, i, c * NC:(c + 1) * NC], ALU.add).then_inc(evac, 1)
                if c == CH - 1:
                    dve.wait_ge(colt, i + 1)
                    dve.tensor_copy(cols[:, i, :, :], pcol[:, 0:4 * KT].rearrange("p (k v) -> p k v", v=2)
                                    ).then_inc(cole, 1)

        @block.tensor
        def _(pe):
            pe.wait_ge(sil, 3)
            for n in range(N):
                i, c = divmod(n, CH)
                pe.wait_ge(wld[n % RING], 16 * (n // RING + 1))
                if n >= 2:
                    pe.wait_ge(evac, n - 1)
                for k in range(KT):
                    x = pe.matmul(pacc[n % 2][0:2, :], csil[:, k, :], w[:, n % RING, k, :],
                                  start=(k == 0), stop=(k == KT - 1))
                x.then_inc(acc, 1)
                if c == CH - 1:
                    pe.wait_ge(evac, n + 1)
                    if i:
                        pe.wait_ge(cole, i)
                    for k in range(2 * KT):
                        x = pe.transpose(pcol[:, 2 * k:2 * k + 2], rows[:, i, k * P:(k + 1) * P], ident[:, :])
                    x.then_inc(colt, 1)


def norm_transpose(nc, a, layer, x_in, mod_cols, mod_rows, h_hi, h_lo):
    R = 3
    with ExitStack() as ctx:
        m = Mem(nc, ctx, f"nt{layer}")
        x = m.sb("x", [P, R, D])
        sq = m.sb("sq", [P, D])
        st = m.sb("st", [P, NCH])
        var = m.sb("var", [P, NCH])
        rstd = m.sb("rstd", [P, NCH])
        mhalf = m.sb("mhalf", [P, 1])
        xn = m.sb("xn", [P, 2, D])
        h32 = m.sb("h32", [P, 2, KT, P])
        preg = m.sb("preg", [P, KT])
        mc = m.sb("mc", [P, 2 * KT, 2])
        gain = m.sb("gain", [P, KT, 2])
        ident = m.sb("ident", [P, P])
        pt = [m.ps(f"pt{i}") for i in range(4)]
        small, con, gn, ssq, vr, rs, nrm, tr, h3, hi, lo = map(
            m.sem, ("small", "con", "gn", "ssq", "vr", "rs", "nrm", "tr", "h3", "hi", "lo"))
        ld = [m.sem(f"ld{i}") for i in range(R)]
        block = ctx.enter_context(nc.Block())

        @block.sync
        def _(sp):
            sp.dma_start(preg[:, :], a["pre_g"][layer]).then_inc(small, 16)
            sp.dma_start(mc[:, :, :], mod_cols[:, layer, :, :]).then_inc(small, 16)
            sp.dma_start(ident[:, :], a["ident"]).then_inc(small, 16)
            for t in range(NCH):
                if t >= R:
                    sp.wait_ge(nrm, t - R + 1)
                sp.dma_start(x[:, t % R, :], x_in(t)).then_inc(ld[t % R], 16)

        @block.scalar
        def _(act):
            def square(t):
                act.wait_ge(ld[t % R], 16 * (t // R + 1))
                if t:
                    act.wait_ge(ssq, t)
                act.activation(sq[:, :], x[:, t % R, :], ACT.Square, accum_out=st[:, t:t + 1]).then_inc(ssq, 1)

            square(0)
            act.wait_ge(gn, 2)
            for t in range(NCH):
                if t + 1 < NCH:
                    square(t + 1)
                v = 1 if t < CCH else 0
                act.wait_ge(tr, t + 1)
                if t >= 2:
                    act.wait_ge(lo, t - 1)
                for k in range(KT):
                    y = act.activation(h32[:, t % 2, k, :], pt[2 * (t % 2) + k // 4][:, (k % 4) * P:(k % 4 + 1) * P],
                                       ACT.Identity, bias=mc[:, k, v:v + 1], scale=gain[:, k, v:v + 1])
                y.then_inc(h3, 1)

        @block.gpsimd
        def _(pool):
            pool.memset(mhalf[:, :], -0.5).then_inc(con, 1)
            pool.wait_ge(con, 1)
            for t in range(NCH):
                pool.wait_ge(vr, t + 1)
                pool.tensor_tensor(rstd[:, t:t + 1], var[:, t:t + 1], mhalf[:, :], ALU.pow).then_inc(rs, 1)

        @block.vector
        def _(dve):
            dve.wait_ge(small, 48)
            dve.tensor_scalar(gain[:, :, :], mc[:, KT:2 * KT, :], 1.0, None, ALU.add).then_inc(gn, 1)
            dve.wait_ge(gn, 1)
            dve.tensor_tensor(gain[:, :, :], gain[:, :, :], preg[:, :].unsqueeze(2).to_broadcast([P, KT, 2]),
                              ALU.mult).then_inc(gn, 1)

            def norm(t):
                dve.wait_ge(ssq, t + 1)
                dve.tensor_scalar(var[:, t:t + 1], st[:, t:t + 1], 1.0 / D, EPS, ALU.mult, ALU.add).then_inc(vr, 1)
                dve.wait_ge(rs, t + 1)
                if t >= 2:
                    dve.wait_ge(tr, t - 1)
                dve.tensor_scalar(xn[:, t % 2, :], x[:, t % R, :], rstd[:, t:t + 1], None, ALU.mult).then_inc(nrm, 1)

            norm(0)
            for t in range(NCH):
                if t + 1 < NCH:
                    norm(t + 1)
                dve.wait_ge(h3, t + 1)
                dve.tensor_copy(h_hi[:, :, t * P:(t + 1) * P], h32[:, t % 2, :, :]).then_inc(hi, 1)
                dve.wait_ge(hi, t + 1)
                dve.tensor_tensor(h_lo[:, :, t * P:(t + 1) * P], h32[:, t % 2, :, :],
                                  h_hi[:, :, t * P:(t + 1) * P].bitcast(F32), ALU.subtract).then_inc(lo, 1)

        @block.tensor
        def _(pe):
            pe.wait_ge(small, 48)
            for t in range(NCH):
                pe.wait_ge(nrm, t + 1)
                if t >= 2:
                    pe.wait_ge(h3, t - 1)
                for k in range(KT):
                    y = pe.transpose(pt[2 * (t % 2) + k // 4][:, (k % 4) * P:(k % 4 + 1) * P],
                                     xn[:, t % 2, k * P:(k + 1) * P], ident[:, :])
                y.then_inc(tr, 1)


def time_steps(nc, a, h_hi, h_lo, tabs_dram):
    H2 = 2 * HEADS
    with ExitStack() as ctx:
        m = Mem(nc, ctx, "ts")
        wr = m.sb("wr", [P, KT, P])
        whi = m.sb("whi", [P, KT, P], F32R)
        wlo = m.sb("wlo", [P, KT, P], F32R)
        raw = m.sb("raw", [P, TOK])
        full = lambda name, dt=F32: m.sb(name, [P, NCH, H2], dt)
        v, e, s, q, dt, av, ahi, alo, cum, dec, ecum, etot, dtdec = map(full, (
            "v", "e", "s", "q", "dt", "av", "ahi", "alo", "cum", "dec", "ecum", "etot", "dtdec"))
        ahr = full("ahr", F32R)
        out = m.sb("out", [P, GROUPS, TABS, NCH, 2 * HPG])
        bias = m.sb("bias", [P, H2])
        alog = m.sb("alog", [P, H2])
        ident, le, ge, ones = (m.sb(n, [P, P]) for n in ("ident", "le", "ge", "ones"))
        pp = [m.ps(f"pp{i}") for i in range(NBL)]
        pT = [m.ps(f"pT{i}") for i in range(2)]
        pc = [m.ps(f"pc{i}") for i in range(2)]
        small, split, pr, rw, tr, vv, ch, ex, cm, tot, pk, st = map(
            m.sem, ("small", "split", "pr", "rw", "tr", "vv", "ch", "ex", "cm", "tot", "pk", "st"))
        block = ctx.enter_context(nc.Block())
        HALF = NCH // 2

        @block.sync
        def _(sp):
            sp.dma_start(wr[:, :, :], a["w_dt"]).then_inc(small, 16)
            sp.dma_start(bias[:, :], a["dt_bias"].partition_broadcast(P)).then_inc(small, 16)
            sp.dma_start(alog[:, :], a["a_log"].partition_broadcast(P)).then_inc(small, 16)
            sp.dma_start(ident[:, :], a["ident"]).then_inc(small, 16)
            sp.dma_start(le[:, :], a["m_le"]).then_inc(small, 16)
            sp.dma_start(ge[:, :], a["m_ge"]).then_inc(small, 16)
            sp.wait_ge(pk, 1)
            sp.dma_start(tabs_dram.rearrange("g p t c h -> p g t c h"), out[:, :, :, :, :]).then_inc(st, 16)
            sp.wait_ge(st, 16)

        @block.gpsimd
        def _(pool):
            pool.memset(ones[:, :], 1.0).then_inc(small, 1)

        @block.scalar
        def _(act):
            act.wait_ge(small, 97)
            act.activation(whi[:, :, :], wr[:, :, :], ACT.Copy).then_inc(split, 1)
            for b, (t0, n) in enumerate(BLOCKS):
                act.wait_ge(pr, b + 1)
                act.activation(raw[:, t0:t0 + n], pp[b][:, 0:n], ACT.Copy).then_inc(rw, 1)
            act.wait_ge(vv, 1)
            act.activation(e[:, :, :], v[:, :, :], ACT.Abs).then_inc(ex, 1)
            act.wait_ge(ex, 1)
            act.activation(e[:, :, :], e[:, :, :], ACT.Exp, scale=-1.0).then_inc(ex, 1)
            act.activation(alog[:, :], alog[:, :], ACT.Exp).then_inc(ex, 1)
            act.wait_ge(cm, 2)
            for i in range(2):
                act.activation(cum[:, :, i * HEADS:(i + 1) * HEADS],
                               pc[i][:, 0:NCH * HEADS].rearrange("p (c h) -> p c h", c=NCH),
                               ACT.Copy).then_inc(ex, 1)
            act.wait_ge(ex, 5)
            act.activation(ecum[:, :, :], cum[:, :, :], ACT.Exp).then_inc(ex, 1)
            act.wait_ge(tot, 2)
            for i in range(2):
                act.activation(etot[:, i * HALF:(i + 1) * HALF, :],
                               pT[i][:, 0:HALF * H2].rearrange("p (c h) -> p c h", h=H2), ACT.Copy).then_inc(ex, 1)
            act.wait_ge(ch, 20)
            act.activation(dec[:, :, :], dec[:, :, :], ACT.Exp).then_inc(ex, 1)
            act.activation(etot[:, :, :], etot[:, :, :], ACT.Exp).then_inc(ex, 1)

        @block.vector
        def _(dve):
            dve.wait_ge(split, 1)
            dve.tensor_tensor(wlo[:, :, :], wr[:, :, :], whi[:, :, :].bitcast(F32), ALU.subtract).then_inc(split, 1)
            dve.wait_ge(tr, 2)
            n = [0]

            def step(x):
                x.then_inc(ch, 1)
                n[0] += 1
                dve.wait_ge(ch, n[0])

            for i in range(2):
                x = dve.tensor_tensor(v[:, i * HALF:(i + 1) * HALF, :],
                                      pT[i][:, 0:HALF * H2].rearrange("p (c h) -> p c h", h=H2),
                                      bias[:, :].unsqueeze(1).to_broadcast([P, HALF, H2]), ALU.add)
            x.then_inc(vv, 1)
            dve.wait_ge(ex, 2)
            step(dve.tensor_scalar(s[:, :, :], e[:, :, :], 2.0, None, ALU.add))
            step(dve.reciprocal(q[:, :, :], s[:, :, :]))
            step(dve.tensor_tensor(s[:, :, :], q[:, :, :], e[:, :, :], ALU.mult))
            step(dve.tensor_tensor(dt[:, :, :], s[:, :, :], s[:, :, :], ALU.mult))
            step(dve.tensor_scalar(q[:, :, :], dt[:, :, :], 1.0 / 17, None, ALU.mult))
            for k in range(15, 1, -2):
                step(dve.scalar_tensor_tensor(q[:, :, :], q[:, :, :], 1.0 / k, dt[:, :, :], ALU.add, ALU.mult))
            step(dve.scalar_tensor_tensor(q[:, :, :], q[:, :, :], 1.0, s[:, :, :], ALU.add, ALU.mult))
            step(dve.tensor_scalar(v[:, :, :], v[:, :, :], 0.0, None, ALU.max))
            step(dve.scalar_tensor_tensor(dt[:, :, :], q[:, :, :], 2.0, v[:, :, :], ALU.mult, ALU.add))
            dve.wait_ge(ex, 3)
            step(dve.scalar_tensor_tensor(av[:, :, :], dt[:, :, :], -1.0,
                                          alog[:, :].unsqueeze(1).to_broadcast([P, NCH, H2]), ALU.mult, ALU.mult))
            step(dve.tensor_copy(ahr[:, :, :], av[:, :, :]))
            step(dve.tensor_copy(ahi[:, :, :], ahr[:, :, :].bitcast(F32)))
            step(dve.tensor_tensor(alo[:, :, :], av[:, :, :], ahi[:, :, :], ALU.subtract))
            assert n[0] == 19
            dve.wait_ge(ex, 8)
            step(dve.tensor_tensor(dec[:, :, :], etot[:, :, :], cum[:, :, :], ALU.subtract))
            dve.wait_ge(ex, 10)
            step(dve.tensor_tensor(dtdec[:, :, :], dt[:, :, :], dec[:, :, :], ALU.mult))
            for i, t in enumerate((ahi, alo, dt, dtdec, ecum, etot)):
                for d in range(2):
                    for g in range(GROUPS):
                        h0 = d * HEADS + g * HPG
                        x = dve.tensor_copy(out[:, g, i, :, d * HPG:(d + 1) * HPG], t[:, :, h0:h0 + HPG])
            x.then_inc(pk, 1)

        @block.tensor
        def _(pe):
            pe.wait_ge(split, 2)
            for b, (t0, n) in enumerate(BLOCKS):
                x = project(pe, pp[b][:, 0:n], whi, wlo, h_hi, h_lo, t0, n)
                x.then_inc(pr, 1)
            pe.wait_ge(rw, NBL)
            for c in range(NCH):
                x = pe.transpose(pT[c // HALF][:, (c % HALF) * H2:(c % HALF + 1) * H2],
                                 raw[0:H2, c * P:(c + 1) * P], ident[0:H2, 0:H2])
                if c % HALF == HALF - 1:
                    x.then_inc(tr, 1)
            pe.wait_ge(ch, 16)
            for i, tri in enumerate((le, ge)):
                pe.matmul(pc[i][:, 0:NCH * HEADS], tri[:, :], av[:, :, i * HEADS:(i + 1) * HEADS],
                          start=True, stop=True).then_inc(cm, 1)
            for i in range(2):
                pe.matmul(pT[i][:, 0:HALF * H2], ones[:, :], av[:, i * HALF:(i + 1) * HALF, :],
                          start=True, stop=True).then_inc(tot, 1)


def project(pe, out, w_hi, w_lo, h_hi, h_lo, t0, n):
    for k in range(KT):
        pe.matmul(out, w_hi[:, k, :], h_hi[:, k, t0:t0 + n], start=(k == 0), stop=False)
        pe.matmul(out, w_hi[:, k, :], h_lo[:, k, t0:t0 + n], start=False, stop=False)
        x = pe.matmul(out, w_lo[:, k, :], h_hi[:, k, t0:t0 + n], start=False, stop=(k == KT - 1))
    return x


def ssd_groups(nc, a, h_hi, h_lo, tabs_dram, y_dram):
    UN = DI // GROUPS
    PAIRS = UN // P
    XT = PAIRS + 2
    B_, C_ = PAIRS, PAIRS + 1
    G = GROUPS
    BACK = list(range(CCH - 1, -1, -1)) + list(range(NCH - 1, CCH - 1, -1))
    H8 = 2 * HPG
    SLOTS = 2 * NCH

    tiles = [("x", 0, i) for i in range(XT)]
    for g in range(G):
        z = [("z", g, i) for i in range(PAIRS)]
        x = [("x", g + 1, i) for i in range(XT)] if g + 1 < G else []
        tiles += x[:1] + z + x[1:]
    w_of = {t: w for w, t in enumerate(tiles)}
    PRO = NBL * XT
    per = NBL * (XT + PAIRS)
    units = {g: [PRO + g * per + s if (g + 1 < G and s < per) or s < NBL * PAIRS else None
                 for s in range(SLOTS)] for g in range(G)}
    x_ready = lambda g: w_of[("x", g, XT - 1)] + 1
    z_ready = lambda g: w_of[("z", g, PAIRS - 1)] + 1

    with ExitStack() as ctx:
        m = Mem(nc, ctx, "sg")
        wr = m.sb("wr", [P, 2, KT, P])
        whi = m.sb("whi", [P, 2, KT, P], F32R)
        wlo = m.sb("wlo", [P, 2, KT, P], F32R)
        u = m.sb("u", [P, UW])
        X = m.sb("X", [P, 2, XT, UW])
        Z = m.sb("Z", [P, PAIRS, TOK])
        tab = m.sb("tab", [P, 2, TABS, NCH, H8])
        hb = m.sb("hb", [P, NCH, UN])
        hf = m.sb("hf", [P, 2, UN])
        cb = m.sb("cb", [P, NCH, P])
        cbm = m.sb("cbm", [P, 2, P])
        hz = m.sb("hz", [P, UN])
        ss = hb[:, :, 0:P]
        aUh = m.sb("aUh", [P, H8, P], F32R)
        aUl = m.sb("aUl", [P, H8, P], F32R)
        E = m.sb("E", [P, H8, P])
        xdt = m.sb("xdt", [P, H8, HD])
        xdb = m.sb("xdb", [P, UN])
        yo = m.sb("yo", [P, H8, HD])
        xD = m.sb("xD", [P, UN])
        sq = m.sb("sq", [P, UN])
        par = m.sb("par", [P, G, XT, 4])
        dsk = m.sb("dsk", [P, 2, UN])
        ng = m.sb("ng", [P, YT])
        ident, le, ge = (m.sb(n, [P, P]) for n in ("ident", "le", "ge"))
        gt = m.sb("gt", [P, P], F32R)
        lt = m.sb("lt", [P, P], F32R)
        mean = m.sb("mean", [P, P])
        eps = m.sb("eps", [P, 1])
        pP = [m.ps(f"pP{i}") for i in range(2)]
        pT, pAf, pAb, pS, pY, pO = (m.ps(n) for n in ("pT", "pAf", "pAb", "pS", "pY", "pO"))

        wld = [m.sem("wld0"), m.sem("wld1")]
        tld = [m.sem("tld0"), m.sem("tld1")]
        (small, con, whs, wls, pj, pev, t0s, cv, tnh, sil, tA, evA, xdA, stA, scA, auh, aul, arg, ex, mm_,
         xdtS, yoff, yoS, yd, xdF, xDs, stF, scF, ysum, fin1, sqs, ssm, ssv, sqr, fin, yst, vch) = map(m.sem, (
             "small", "con", "whs", "wls", "pj", "pev", "t0s", "cv", "tnh", "sil", "tA", "evA", "xdA", "stA",
             "scA", "auh", "aul", "arg", "ex", "mm", "xdtS", "yoff", "yoS", "yd", "xdF", "xDs", "stF", "scF",
             "ysum", "fin1", "sqs", "ssm", "ssv", "sqr", "fin", "yst", "vch"))
        block = ctx.enter_context(nc.Block())

        def xt(g, c):
            return X[:, g % 2, 0:PAIRS, ucol(c * P):ucol(c * P) + P]

        def heads(ap):
            return ap.rearrange("p (t h) c -> p t h c", t=PAIRS)

        def xth(g, c):
            return xt(g, c).rearrange("p t (h c) -> p t h c", c=HD)

        def col(g, which, c, lo, n=HPG):
            return tab[:, g % 2, which, c, lo:lo + n].unsqueeze(2).to_broadcast([P, n, HD])

        @block.sync
        def _(sp):
            for dst, src in ((par, "conv"), (ng, "norm_g"), (ident, "ident"), (le, "m_le"),
                             (ge, "m_ge")):
                sp.dma_start(dst[tuple(slice(None) for _ in dst.shape)], a[src]).then_inc(small, 16)

            def tables(g):
                sp.dma_start(tab[:, g % 2, :, :, :], tabs_dram[g]).then_inc(tld[g % 2], 16)
                sp.dma_start(dsk[:, g % 2, :], a["dskip"][g * UN:(g + 1) * UN].partition_broadcast(P)
                             ).then_inc(tld[g % 2], 16)

            for w, (kind, g, i) in enumerate(tiles):
                if w >= 2:
                    sp.wait_ge(wls, w - 1)
                sp.dma_start(wr[:, w % 2, :, :], a["w_ssd"][w]).then_inc(wld[w % 2], 16)
                if w == 1:
                    tables(0)
                    tables(1)
                if kind == "z" and i == 0 and g >= 1:
                    sp.wait_ge(fin, g)
                    sp.dma_start(y_dram[:, 2 * (g - 1):2 * g, :], Z[:, :, :]).then_inc(yst, 16)
                    if g + 1 < G:
                        tables(g + 1)
            sp.wait_ge(fin, G)
            sp.dma_start(y_dram[:, 2 * (G - 1):2 * G, :], Z[:, :, :]).then_inc(yst, 16)
            sp.wait_ge(yst, 16 * G)

        @block.tensor
        def _(pe):
            def unit(q):
                w, b = divmod(q, NBL)
                t0, n = BLOCKS[b]
                pe.wait_ge(wls, w + 1)
                if q >= 2:
                    pe.wait_ge(pev, q - 1)
                project(pe, pP[q % 2][:, 0:n], whi[:, w % 2], wlo[:, w % 2], h_hi, h_lo, t0, n).then_inc(pj, 1)

            def args(g, c):
                i = g * NCH + c
                pe.wait_ge(auh, i + 1)
                pe.wait_ge(aul, i + 1)
                if i:
                    pe.wait_ge(ex, i)
                for d, (bank, tri) in enumerate(((pAf, gt), (pAb, lt))):
                    for part, au in enumerate((aUh, aUl)):
                        x = pe.matmul(bank[:, :], tri[:, :], au[:, d * HPG:(d + 1) * HPG, :]
                                      .rearrange("p h l -> p (h l)"), start=(part == 0), stop=(part == 1))
                x.then_inc(arg, 1)

            def back(g, i):
                c = BACK[i]
                n = g * NCH + i
                u0 = ucol(c * P)
                if i == 0:
                    pe.wait_ge(sil, x_ready(g))
                    if g:
                        pe.wait_ge(ssv, g * NCH)
                if n:
                    pe.wait_ge(evA, n)
                for t in range(XT - 1):
                    pe.transpose(pT[:, t * P:(t + 1) * P], X[:, g % 2, t, u0:u0 + P], ident[:, :])
                pe.matmul(pT[:, 3 * P:4 * P], X[:, g % 2, B_, u0:u0 + P], X[:, g % 2, C_, u0:u0 + P],
                          start=True, stop=True).then_inc(tA, 1)

            def back_state(g, i):
                n = g * (NCH - 1) + i
                u0 = ucol(BACK[i] * P)
                pe.wait_ge(xdA, n + 1)
                if n:
                    pe.wait_ge(scA, n)
                if g:
                    pe.wait_ge(scF, g * (NCH - 1))
                pe.matmul(pS[:, 0:UN], X[:, g % 2, B_, u0:u0 + P], xdb[:, :], start=True, stop=True).then_inc(stA, 1)

            def forth(g, c):
                n = g * NCH + c
                u0 = ucol(c * P)
                if c + 1 < NCH:
                    args(g, c + 1)
                if c:
                    pe.wait_ge(scF, g * (NCH - 1) + c)
                else:
                    pe.wait_ge(scA, (g + 1) * (NCH - 1))
                if n:
                    pe.wait_ge(yoS, n)
                prev = hf[:, c % 2, :] if c else hz[:, :]
                back = hz[:, :] if c == CCH - 1 else hb[:, c, :]
                pe.matmul(pO[:, 0:UN], X[:, g % 2, C_, u0:u0 + P], prev, start=True, stop=True)
                pe.matmul(pO[:, UN:2 * UN], X[:, g % 2, C_, u0:u0 + P], back, start=True,
                          stop=True).then_inc(yoff, 1)
                pe.wait_ge(mm_, n + 1)
                pe.wait_ge(xdtS, n + 1)
                if n:
                    pe.wait_ge(fin1, n)
                for k in range(HPG):
                    r = (k % 2) * HD
                    for d in range(2):
                        x = pe.matmul(pY[r:r + HD, (k // 2) * P:(k // 2 + 1) * P], xdt[:, d * HPG + k, :],
                                      E[:, d * HPG + k, :], start=(k < 2 and d == 0), stop=False,
                                      skip_group_check=True)
                x.then_inc(yd, 1)
                if c + 1 < NCH:
                    pe.wait_ge(xdF, g * (NCH - 1) + c + 1)
                    if c:
                        pe.wait_ge(scF, g * (NCH - 1) + c)
                    pe.matmul(pS[:, 0:UN], X[:, g % 2, B_, u0:u0 + P], xdb[:, :], start=True,
                              stop=True).then_inc(stF, 1)

            def off_sum(g, c):
                n = g * NCH + c
                pe.wait_ge(yoS, n + 1)
                for t in range(PAIRS):
                    x = pe.matmul(pY[:, t * P:(t + 1) * P], yo[:, 2 * t:2 * t + 2, :].rearrange("p h c -> p (h c)"),
                                  ident[:, :], start=False, stop=(t == PAIRS - 1), skip_group_check=True)
                x.then_inc(ysum, 1)

            def squares(g, c):
                n = g * NCH + c
                pe.wait_ge(sqs, n + 1)
                if c:
                    pe.wait_ge(ssv, n)
                for t in range(PAIRS):
                    x = pe.matmul(pT[:, 0:P], mean[:, :], sq[:, t * P:(t + 1) * P], start=(t == 0),
                                  stop=(t == PAIRS - 1))
                x.then_inc(ssm, 1)

            pe.wait_ge(small, 80)
            pe.wait_ge(con, 6)
            for q in range(PRO):
                unit(q)
            for g in range(G):
                for i in range(NCH):
                    back(g, i)
                    if units[g][i] is not None:
                        unit(units[g][i])
                    if i < NCH - 1:
                        back_state(g, i)
                args(g, 0)
                for c in range(NCH):
                    forth(g, c)
                    if units[g][NCH + c] is not None:
                        unit(units[g][NCH + c])
                    off_sum(g, c)
                    if c:
                        squares(g, c - 1)
                squares(g, NCH - 1)

        @block.scalar
        def _(act):
            def split(w):
                act.wait_ge(wld[w % 2], 16 * (w // 2 + 1))
                if w >= 2:
                    act.wait_ge(pj, NBL * (w - 1))
                act.activation(whi[:, w % 2, :, :], wr[:, w % 2, :, :], ACT.Copy).then_inc(whs, 1)

            def take(q):
                w, b = divmod(q, NBL)
                kind, g, i = tiles[w]
                t0, n = BLOCKS[b]
                act.wait_ge(pj, q + 1)
                if kind == "x":
                    if b == 0 and w:
                        act.wait_ge(sil, w)
                    act.activation(u[:, ucol(t0):ucol(t0) + n], pP[q % 2][:, 0:n], ACT.Copy).then_inc(pev, 1)
                else:
                    if b == 0 and i == 0 and g:
                        act.wait_ge(yst, 16 * g)
                    act.activation(Z[:, i, t0:t0 + n], pP[q % 2][:, 0:n], ACT.Copy, scale=0.5).then_inc(pev, 1)
                if b == 0 and w + 1 < len(tiles):
                    split(w + 1)
                if b == NBL - 1 and kind == "x":
                    act.wait_ge(pev, q + 1)
                    act.activation(X[:, g % 2, i, 1:UW - 1], u[:, 1:UW - 1], ACT.Identity,
                                   bias=par[:, g, i, 3:4], scale=par[:, g, i, 1:2]).then_inc(t0s, 1)

            def gate(w):
                kind, g, i = tiles[w]
                if kind == "x":
                    act.wait_ge(cv, 2 * (w_x[w] + 1))
                    act.activation(u[:, 1:UW - 1], X[:, g % 2, i, 1:UW - 1], ACT.Tanh).then_inc(tnh, 1)
                else:
                    act.wait_ge(pev, NBL * (w + 1))
                    if w:
                        act.wait_ge(sil, w)
                    act.activation(u[:, 1:TOK + 1], Z[:, i, :], ACT.Tanh).then_inc(tnh, 1)

            def steps_hi(g, c):
                n = g * NCH + c
                if c == 0:
                    act.wait_ge(tld[g % 2], 32 * (g // 2 + 1))
                if n:
                    act.wait_ge(arg, n)
                for k in range(H8):
                    x = act.activation(aUh[:, k, :], (le if k < HPG else ge)[:, :], ACT.Copy,
                                       scale=tab[:, g % 2, A_HI, c, k:k + 1])
                x.then_inc(auh, 1)

            def back(g, i):
                c = BACK[i]
                u0 = ucol(c * P)
                n = g * NCH + i
                act.wait_ge(tA, n + 1)
                act.activation(X[:, g % 2, 0:XT - 1, u0:u0 + P], pT[:, 0:3 * P].rearrange("p (t c) -> p t c", c=P),
                               ACT.Copy)
                if g and i == 0:
                    act.wait_ge(mm_, g * NCH)
                act.activation(cb[:, c, :], pT[:, 3 * P:4 * P], ACT.Copy).then_inc(evA, 1)

            def decays(g, c):
                n = g * NCH + c
                act.wait_ge(arg, n + 1)
                if n:
                    act.wait_ge(yd, n)
                act.activation(E[:, 0:HPG, :], pAf[:, :].rearrange("p (h l) -> p h l", l=P), ACT.Exp)
                act.activation(E[:, HPG:H8, :], pAb[:, :].rearrange("p (h l) -> p h l", l=P), ACT.Exp).then_inc(ex, 1)

            def square(g, c):
                n = g * NCH + c
                act.wait_ge(fin1, n + 1)
                if n:
                    act.wait_ge(ssm, n)
                act.activation(sq[:, :].rearrange("p (t l) -> p t l", l=P), Z[:, :, c * P:(c + 1) * P],
                               ACT.Square).then_inc(sqs, 1)

            def keep_sum(g, c):
                n = g * NCH + c
                act.wait_ge(ssm, n + 1)
                if c == 0 and g:
                    act.wait_ge(fin, g)
                act.activation(ss[:, c, :], pT[:, 0:P], ACT.Copy).then_inc(ssv, 1)

            w_x = {w: n for n, w in enumerate([w for w, t in enumerate(tiles) if t[0] == "x"])}
            act.wait_ge(small, 80)
            act.wait_ge(con, 6)
            split(0)
            for q in range(PRO):
                take(q)
                if q % NBL == NBL - 1:
                    gate(q // NBL)
            pend = None
            for g in range(G):
                for s in range(SLOTS):
                    q = units[g][s]
                    c = s - NCH
                    if c < 0:
                        back(g, s)
                        if s == NCH - 1:
                            steps_hi(g, 0)
                    if pend is not None:
                        gate(pend)
                        pend = None
                    if c == 0:
                        decays(g, 0)
                        steps_hi(g, 1)
                    if c >= 0 and c + 1 < NCH:
                        decays(g, c + 1)
                        if c + 2 < NCH:
                            steps_hi(g, c + 2)
                    if c > 0:
                        square(g, c - 1)
                    if q is not None:
                        take(q)
                        if q % NBL == NBL - 1:
                            pend = q // NBL
                    if c > 0:
                        keep_sum(g, c - 1)
                square(g, NCH - 1)
                keep_sum(g, NCH - 1)
                act.wait_ge(ssv, (g + 1) * NCH)
                act.activation(ss, ss, ACT.Sqrt, bias=eps[:, 0:1]).then_inc(sqr, 1)

        @block.gpsimd
        def _(pool):
            pool.memset(mean[:, :], 1.0 / UN).then_inc(con, 1)
            pool.memset(eps[:, :], EPS).then_inc(con, 1)

            def split_lo(w):
                pool.wait_ge(whs, w + 1)
                pool.tensor_tensor(wlo[:, w % 2, :, :], wr[:, w % 2, :, :], whi[:, w % 2, :, :].bitcast(F32),
                                   ALU.subtract).then_inc(wls, 1)

            split_lo(0)
            for q in range(PRO):
                if q % NBL == 0:
                    split_lo(q // NBL + 1)
            for g in range(G):
                for s in range(SLOTS):
                    c = s - NCH
                    if c < 0 and s < NCH - 1:
                        n = g * (NCH - 1) + s
                        pool.wait_ge(evA, g * NCH + s + 1)
                        if s == 0:
                            pool.wait_ge(tld[g % 2], 32 * (g // 2 + 1))
                            if g:
                                pool.wait_ge(stF, g * (NCH - 1))
                        if n:
                            pool.wait_ge(stA, n)
                        cc = BACK[s]
                        pool.tensor_tensor(heads(xdb[:, :].rearrange("p (h c) -> p h c", c=HD)), xth(g, cc),
                                           heads(col(g, DTDEC, cc, HPG)), ALU.mult).then_inc(xdA, 1)
                    if c == 0:
                        pool.wait_ge(evA, (g + 1) * NCH)
                    if c >= 0:
                        if c + 1 < NCH:
                            n = g * (NCH - 1) + c
                            if c == 0:
                                pool.wait_ge(stA, (g + 1) * (NCH - 1))
                            if n:
                                pool.wait_ge(stF, n)
                            pool.tensor_tensor(heads(xdb[:, :].rearrange("p (h c) -> p h c", c=HD)), xth(g, c),
                                               heads(col(g, DTDEC, c, 0)), ALU.mult).then_inc(xdF, 1)
                        n = g * NCH + c
                        if n:
                            pool.wait_ge(yoS, n)
                        pool.tensor_tensor(xD[:, :].rearrange("p (t c) -> p t c", c=P), xt(g, c),
                                           dsk[:, g % 2, :].rearrange("p (t c) -> p t c", c=P),
                                           ALU.mult).then_inc(xDs, 1)
                    q = units[g][s]
                    if q is not None and q % NBL == 0 and q // NBL + 1 < len(tiles):
                        split_lo(q // NBL + 1)

        @block.vector
        def _(dve):
            n_ch = [0]

            def chain(x):
                x.then_inc(vch, 1)
                n_ch[0] += 1
                dve.wait_ge(vch, n_ch[0])

            for x in (dve.memset(u[:, :], 0.0), dve.memset(hz[:, :], 0.0)):
                x.then_inc(con, 1)
            dve.wait_ge(small, 80)
            chain(dve.tensor_scalar(par[:, :, :, :], par[:, :, :, :], 0.5, None, ALU.mult))
            dve.tensor_scalar(gt[:, :], le[:, :], -1.0, 1.0, ALU.mult, ALU.add).then_inc(con, 1)
            dve.tensor_scalar(lt[:, :], ge[:, :], -1.0, 1.0, ALU.mult, ALU.add).then_inc(con, 1)

            nx = [0]

            def conv(w):
                kind, g, i = tiles[w]
                if kind != "x":
                    return
                dve.wait_ge(t0s, nx[0] + 1)
                o = X[:, g % 2, i, 1:UW - 1]
                for tap, src in ((0, u[:, 0:UW - 2]), (2, u[:, 2:UW])):
                    dve.scalar_tensor_tensor(o, src, par[:, g, i, tap:tap + 1], o, ALU.mult, ALU.add).then_inc(cv, 1)
                    if tap == 0:
                        dve.wait_ge(cv, 2 * nx[0] + 1)
                nx[0] += 1

            def silu(w):
                kind, g, i = tiles[w]
                dve.wait_ge(tnh, w + 1)
                if kind == "x":
                    o, t = X[:, g % 2, i, 1:UW - 1], u[:, 1:UW - 1]
                else:
                    o, t = Z[:, i, :], u[:, 1:TOK + 1]
                chain(dve.scalar_tensor_tensor(o, t, 1.0, o, ALU.add, ALU.mult))
                dve.memset(u[:, ucol(CTX) - 2:ucol(CTX)], 0.0).then_inc(sil, 1)

            def steps_lo(g, c):
                n = g * NCH + c
                if c == 0:
                    dve.wait_ge(tld[g % 2], 32 * (g // 2 + 1))
                if n:
                    dve.wait_ge(arg, n)
                for k in range(H8):
                    x = dve.tensor_scalar(aUl[:, k, :], (le if k < HPG else ge)[:, :],
                                          tab[:, g % 2, A_LO, c, k:k + 1], None, ALU.mult)
                x.then_inc(aul, 1)

            def h3(ap):
                return ap.rearrange("p (h c) -> p h c", c=HD)

            def back(g, i):
                if i == NCH - 1:
                    return
                n = g * (NCH - 1) + i
                c, nxt = BACK[i], BACK[i + 1]
                if i == 0 and g:
                    dve.wait_ge(yoff, g * NCH)
                    dve.wait_ge(fin, g)
                if i == 0:
                    dve.wait_ge(tld[g % 2], 32 * (g // 2 + 1))
                if n:
                    dve.wait_ge(scA, n)
                chain(dve.tensor_tensor(h3(hb[:, nxt, :]), h3(hb[:, c, :] if i else hz[:, :]),
                                        col(g, ETOT, c, HPG), ALU.mult))
                dve.wait_ge(stA, n + 1)
                dve.tensor_tensor(hb[:, nxt, :], hb[:, nxt, :], pS[:, 0:UN], ALU.add).then_inc(scA, 1)

            def xdts(g, c):
                n = g * NCH + c
                if c == 0:
                    dve.wait_ge(evA, (g + 1) * NCH)
                if n:
                    dve.wait_ge(yd, n)
                for d in range(2):
                    x = dve.tensor_tensor(heads(xdt[:, d * HPG:(d + 1) * HPG, :]), xth(g, c),
                                          heads(col(g, DT, c, d * HPG)), ALU.mult)
                x.then_inc(xdtS, 1)

            def masks(g, c):
                n = g * NCH + c
                dve.wait_ge(evA, (g + 1) * NCH)
                for d, tri in enumerate((le, ge)):
                    x = dve.tensor_tensor(cbm[:, d, :], cb[:, c, :], tri[:, :], ALU.mult)
                chain(x)
                dve.wait_ge(ex, n + 1)
                for d in range(2):
                    x = dve.tensor_tensor(E[:, d * HPG:(d + 1) * HPG, :], E[:, d * HPG:(d + 1) * HPG, :],
                                          cbm[:, d, :].unsqueeze(1).to_broadcast([P, HPG, P]), ALU.mult)
                x.then_inc(mm_, 1)

            def offs(g, c):
                n = g * NCH + c
                dve.wait_ge(yoff, n + 1)
                if n:
                    dve.wait_ge(ysum, n)
                chain(dve.tensor_tensor(yo[:, :, :], pO[:, :].rearrange("p (h c) -> p h c", c=HD),
                                        col(g, ECUM, c, 0, H8), ALU.mult))
                chain(dve.tensor_tensor(yo[:, 0:HPG, :], yo[:, 0:HPG, :], yo[:, HPG:H8, :], ALU.add))
                dve.wait_ge(xDs, n + 1)
                dve.tensor_tensor(yo[:, 0:HPG, :], yo[:, 0:HPG, :], h3(xD[:, :]), ALU.add).then_inc(yoS, 1)

            def scan(g, c):
                if c == NCH - 1:
                    return
                n = g * (NCH - 1) + c
                prev = hf[:, c % 2, :] if c else hz[:, :]
                nxt = hf[:, (c + 1) % 2, :]
                if n:
                    dve.wait_ge(scF, n)
                chain(dve.tensor_tensor(h3(nxt), h3(prev), col(g, ETOT, c, 0), ALU.mult))
                dve.wait_ge(stF, n + 1)
                dve.tensor_tensor(nxt, nxt, pS[:, 0:UN], ALU.add).then_inc(scF, 1)

            def gated(g, c):
                n = g * NCH + c
                dve.wait_ge(ysum, n + 1)
                zc = Z[:, :, c * P:(c + 1) * P]
                dve.tensor_tensor(zc, pY[:, 0:UN].rearrange("p (t l) -> p t l", l=P), zc, ALU.mult).then_inc(fin1, 1)

            for w in range(XT):
                conv(w)
                silu(w)
            pend = None
            for g in range(G):
                for s in range(SLOTS):
                    q = units[g][s]
                    c = s - NCH
                    if pend is not None:
                        silu(pend)
                        pend = None
                    if c < 0:
                        back(g, s)
                        if s == NCH - 1:
                            steps_lo(g, 0)
                            xdts(g, 0)
                    if c == 0:
                        masks(g, 0)
                        steps_lo(g, 1)
                    if c >= 0:
                        offs(g, c)
                        scan(g, c)
                        if c + 1 < NCH:
                            masks(g, c + 1)
                            xdts(g, c + 1)
                            if c + 2 < NCH:
                                steps_lo(g, c + 2)
                        gated(g, c)
                    if q is not None and q % NBL == NBL - 1:
                        conv(q // NBL)
                        pend = q // NBL
                dve.wait_ge(sqr, g + 1)
                chain(dve.reciprocal(ss, ss))
                for t in range(PAIRS):
                    zt = Z[:, t, :].rearrange("p (c l) -> p c l", l=P)
                    x = dve.scalar_tensor_tensor(zt, zt, ng[:, g * PAIRS + t:g * PAIRS + t + 1], ss,
                                                 ALU.mult, ALU.mult)
                x.then_inc(fin, 1)


def out_project(nc, a, layer, y_dram, kt, w_dram, tiles, mod_rows, st_o):
    NH = D // 2
    with ExitStack() as ctx:
        m = Mem(nc, ctx, f"op{layer}")
        whi = m.sb("whi", [P, kt, D], F32R)
        wlo = m.sb("wlo", [P, kt, D], F32R)
        wr = m.sb("wr", [P, 2, D])
        yr = m.sb("yr", [P, 2, kt, P])
        yhi = m.sb("yhi", [P, 2, kt, P], F32R)
        ylo = m.sb("ylo", [P, 2, kt, P], F32R)
        x = m.sb("x", [P, 2, D])
        o = m.sb("o", [P, D])
        G = m.sb("G", [P, 2, D])
        st = m.sb("st", [P, 2])
        var = m.sb("var", [P, 1])
        rstd = m.sb("rstd", [P, 1])
        mhalf = m.sb("mhalf", [P, 1])
        pa = [[m.ps(f"pa{i}{h}") for h in range(2)] for i in range(2)]
        wl = [m.sem("wl0"), m.sem("wl1")]
        yl = [m.sem("yl0"), m.sem("yl1")]
        xl = [m.sem("xl0"), m.sem("xl1")]
        gl, gg, whs, wls, yhs, yls, mm_, sqs, vr, rs, sc, ad, con = map(m.sem, (
            "gl", "gg", "whs", "wls", "yhs", "yls", "mm", "sqs", "vr", "rs", "sc", "ad", "con"))
        block = ctx.enter_context(nc.Block())
        N = len(tiles)

        @block.sync
        def _(sp):
            def load_y(t):
                if t >= 2:
                    sp.wait_ge(yls, t - 1)
                c0 = tiles[t][0]
                sp.dma_start(yr[:, t % 2, :, :], y_dram[:, :, c0:c0 + P]).then_inc(yl[t % 2], 16)

            for k in range(kt):
                if k >= 2:
                    sp.wait_ge(wls, k - 1)
                sp.dma_start(wr[:, k % 2, :], w_dram[k * P:(k + 1) * P, :]).then_inc(wl[k % 2], 16)
                if k == 0:
                    load_y(0)
            sp.dma_start(o[:, :], a["post_g"][layer].partition_broadcast(P)).then_inc(gl, 16)
            for v in range(2):
                sp.dma_start(G[:, v, :], mod_rows[v, layer, 2 * D:3 * D].partition_broadcast(P)).then_inc(gl, 16)
            load_y(1)
            for t in range(N):
                if t >= 2:
                    sp.wait_ge(ad, t - 1)
                (dst, src) = tiles[t][2](x[:, t % 2, :])
                sp.dma_start(dst, src).then_inc(xl[t % 2], 16)
                if t >= 1:
                    if t + 1 < N:
                        load_y(t + 1)
                    sp.wait_ge(ad, t)
                    (dst, src) = tiles[t - 1][3](o[:, :])
                    sp.dma_start(dst, src).then_inc(st_o, 16)
            sp.wait_ge(ad, N)
            (dst, src) = tiles[N - 1][3](o[:, :])
            sp.dma_start(dst, src).then_inc(st_o, 16)
            sp.wait_ge(st_o, 16 * N)

        @block.tensor
        def _(pe):
            for t in range(N):
                pe.wait_ge(yls, t + 1)
                if t >= 2:
                    pe.wait_ge(sc, 2 * (t - 1))
                for k in range(kt):
                    if t == 0:
                        pe.wait_ge(wls, k + 1)
                    for y, ws in ((yhi, (whi, wlo)), (ylo, (whi,))):
                        for w in ws:
                            for h in range(2):
                                z = pe.matmul(pa[t % 2][h][:, :], y[:, t % 2, k, :], w[:, k, h * NH:(h + 1) * NH],
                                              start=(k == 0 and y is yhi and w is whi),
                                              stop=(k == kt - 1 and y is ylo))
                z.then_inc(mm_, 1)

        @block.scalar
        def _(act):
            def y_hi(t):
                act.wait_ge(yl[t % 2], 16 * (t // 2 + 1))
                if t >= 2:
                    act.wait_ge(mm_, t - 1)
                act.activation(yhi[:, t % 2, :, :], yr[:, t % 2, :, :], ACT.Copy).then_inc(yhs, 1)

            for k in range(kt):
                act.wait_ge(wl[k % 2], 16 * (k // 2 + 1))
                act.activation(whi[:, k, :], wr[:, k % 2, :], ACT.Copy).then_inc(whs, 1)
                if k == 0:
                    y_hi(0)
            y_hi(1)
            for t in range(N):
                act.wait_ge(mm_, t + 1)
                if t:
                    act.wait_ge(st_o, 16 * t)
                else:
                    act.wait_ge(gg, 1)
                for h in range(2):
                    z = act.activation(o[:, h * NH:(h + 1) * NH], pa[t % 2][h][:, :], ACT.Square,
                                       accum_out=st[:, h:h + 1])
                z.then_inc(sqs, 1)
                if t + 2 < N:
                    y_hi(t + 2)

        @block.gpsimd
        def _(pool):
            pool.memset(mhalf[:, :], -0.5).then_inc(con, 1)
            pool.wait_ge(con, 1)
            for t in range(N):
                pool.wait_ge(vr, 2 * t + 2)
                pool.tensor_tensor(rstd[:, :], var[:, :], mhalf[:, :], ALU.pow).then_inc(rs, 1)

        @block.vector
        def _(dve):
            def y_lo(t):
                dve.wait_ge(yhs, t + 1)
                dve.tensor_tensor(ylo[:, t % 2, :, :], yr[:, t % 2, :, :], yhi[:, t % 2, :, :].bitcast(F32),
                                  ALU.subtract).then_inc(yls, 1)

            for k in range(kt):
                dve.wait_ge(whs, k + 1)
                dve.tensor_tensor(wlo[:, k, :], wr[:, k % 2, :], whi[:, k, :].bitcast(F32),
                                  ALU.subtract).then_inc(wls, 1)
                if k == 0:
                    y_lo(0)
            dve.wait_ge(gl, 48)
            dve.tensor_tensor(G[:, :, :], G[:, :, :], o[:, :].unsqueeze(1).to_broadcast([P, 2, D]),
                              ALU.mult).then_inc(gg, 1)
            y_lo(1)
            for t in range(N):
                v = 1 if tiles[t][1] else 0
                dve.wait_ge(sqs, t + 1)
                dve.tensor_tensor(var[:, :], st[:, 0:1], st[:, 1:2], ALU.add).then_inc(vr, 1)
                dve.wait_ge(vr, 2 * t + 1)
                dve.tensor_scalar(var[:, :], var[:, :], 1.0 / D, EPS, ALU.mult, ALU.add).then_inc(vr, 1)
                dve.wait_ge(rs, t + 1)
                if t == 0:
                    dve.wait_ge(gg, 1)
                for h in range(2):
                    dve.scalar_tensor_tensor(o[:, h * NH:(h + 1) * NH], pa[t % 2][h][:, :], rstd[:, 0:1],
                                             G[:, v, h * NH:(h + 1) * NH], ALU.mult, ALU.mult).then_inc(sc, 1)
                dve.wait_ge(sc, 2 * (t + 1))
                dve.wait_ge(xl[t % 2], 16 * (t // 2 + 1))
                dve.tensor_tensor(o[:, :], o[:, :], x[:, t % 2, :], ALU.add).then_inc(ad, 1)
                if t + 2 < N:
                    y_lo(t + 2)


GW, WR, WC = 64, 8, 16
GR = SEQ // GW
NAH, NAD = 16, 64
QR, QC = 8, 16
RB, CB = GR // QR, GW // QC
KR, KC = 12, 32
DR, DC = 2 * WR - 1, 2 * WC - 1
K0C = [min(max(QC * c - WC // 2, 0), GW - KC) for c in range(CB)]
NEG = -1e30
PADW = 64


def key_row0(rb):
    return (WR // 2) * rb


def row_start(r):
    return min(max(r - WR // 2, 0), GR - WR)


def bias_tables(nc, a, pad_dram, bt_dram):
    NR = NAH * DR
    with ExitStack() as ctx:
        m = Mem(nc, ctx, "bt")
        rows = [m.sb(f"rows{i}", [NR // 2, PADW]) for i in range(2)]
        T = m.sb("T", [CB * QC, NR, KC])
        mask = m.sb("mask", [CB * QC, KC])
        z, ld, pd, wn, ad, st = map(m.sem, ("z", "ld", "pd", "wn", "ad", "st"))
        block = ctx.enter_context(nc.Block())

        @block.vector
        def _(dve):
            for i in range(2):
                dve.memset(rows[i][:, :], 0.0).then_inc(z, 1)
            dve.wait_ge(wn, 16 * (CB * QC + 1))
            dve.tensor_tensor(T[:, :, :], T[:, :, :], mask[:, :].unsqueeze(1).to_broadcast([CB * QC, NR, KC]),
                              ALU.add).then_inc(ad, 1)

        @block.sync
        def _(sp):
            sp.wait_ge(z, 2)
            for i in range(2):
                sp.dma_start(rows[i][:, QC:QC + DC], a["rpb"][i * NR // 2:(i + 1) * NR // 2, :]).then_inc(ld, 16)
            sp.wait_ge(ld, 32)
            for i in range(2):
                sp.dma_start(pad_dram[i * NR // 2:(i + 1) * NR // 2, :], rows[i][:, :]).then_inc(pd, 16)
            sp.wait_ge(pd, 32)
            sp.dma_start(mask[:, :], a["colmask"]).then_inc(wn, 16)
            for c in range(CB):
                for q in range(QC):
                    first = QC + WC - 1 + K0C[c] - QC * c - q
                    sp.dma_start(T[c * QC + q:c * QC + q + 1, :, :],
                                 pad_dram[:, first:first + KC].unsqueeze(0)).then_inc(wn, 16)
            sp.wait_ge(ad, 1)
            sp.dma_start(bt_dram, T[:, :, :]).then_inc(st, 16)
            sp.wait_ge(st, 16)


def attention(nc, a, h_hi, h_lo, bt_dram, y_dram):
    PR = NAH // 2
    QT = RB * CB
    UP = 2 * QT
    NU = PR * UP
    NW, NC_ = KR * KC, CTX
    NK = NW + NC_
    JW, JC = NW // P, NC_ // P
    WIN = CB * (GR // 4)
    KINDS = "vkqg"
    ublocks = {"v": (0, 1, 2), "k": (0, 1, 2), "q": (1, 2), "g": (1, 2)}
    units = [(p, i, kd, b) for p in range(PR) for i, kd in enumerate(KINDS) for b in ublocks[kd]]
    UPP = len(units) // PR
    place = {i * UP // UPP: i for i in range(UPP)}
    done = {}
    for q, (p, i, kd, b) in enumerate(units):
        done[p, kd] = q + 1
    VG = -(-(WIN + JC) // 4)
    VS = UP - VG

    with ExitStack() as ctx:
        m = Mem(nc, ctx, "at")
        wr = m.sb("wr", [P, 2, KT, P])
        whi = m.sb("whi", [P, 2, KT, P], F32R)
        wlo = m.sb("wlo", [P, 2, KT, P], F32R)
        q2 = m.sb("q2", [P, 2, 2, SEQ])
        kk = m.sb("kk", [P, 2, TOK])
        vv = m.sb("vv", [P, WIN + JC, P])
        vt = m.sb("vt", [P, 2, WIN + JC, P])
        gg = m.sb("gg", [P, 2, SEQ])
        th = m.sb("th", [P, SEQ])
        bias = m.sb("bias", [P, RB, 2, CB, KR, KC])
        s = m.sb("s", [P, 2, NW])
        pm = m.sb("pm", [P, 2, NK])
        ptr = m.sb("ptr", [P, 2, JW + JC, P])
        ident = m.sb("ident", [P, P])
        mx = m.sb("mx", [P, 2, 2])
        nm = m.sb("nm", [P, 2])
        lsum = m.sb("lsum", [P, 2, 2])
        li = m.sb("li", [P, 2])
        pP = [m.ps(f"pP{i}") for i in range(2)]
        pA, pB, pT0, pT1, pO = (m.ps(n) for n in ("pA", "pB", "pT0", "pT1", "pO"))
        wld = [m.sem("wld0"), m.sem("wld1")]
        bl = [m.sem("bl0"), m.sem("bl1")]
        (small, con, whs, wls, pj, pev, tnh, gs, sc, mxs, nms, exs, ls, pn, tr, pt0, pt1, pv, ga, vtr, vte,
         yst) = map(m.sem, (
             "small", "con", "whs", "wls", "pj", "pev", "tnh", "gs", "sc", "mxs", "nms", "exs", "ls", "pn", "tr",
             "pt0", "pt1", "pv", "ga", "vtr", "vte", "yst"))
        block = ctx.enter_context(nc.Block())
        bview = bt_dram.rearrange("(c q) (h r) k -> q h c (r k)", c=CB, r=DR)

        def grid(ap):
            return ap[:, CTX:TOK].rearrange("p (r c) -> p r c", c=GW)

        def rest(n):
            p, r = divmod(n, UP)
            qt, e = divmod(r, 2)
            return p, qt, e, qt // CB, qt % CB

        def win_index(rb, cb, j):
            return cb * (GR // 4) + rb + j if j < JW else WIN + j - JW

        @block.sync
        def _(sp):
            sp.dma_start(ident[:, :], a["ident"]).then_inc(small, 16)

            def load_bias(p, rb):
                if p:
                    sp.wait_ge(mxs, p * UP - UP + (rb + 1) * UP // RB)
                for e in range(2):
                    for qr in range(QR):
                        r = rb * QR + qr
                        k0 = row_start(r) - key_row0(rb)
                        d0 = row_start(r) - r + WR - 1
                        sp.dma_start(bias[qr * QC:(qr + 1) * QC, rb, e, :, k0:k0 + WR, :]
                                     .rearrange("q c r k -> q c (r k)"),
                                     bview[:, 2 * p + e, :, d0 * KC:(d0 + WR) * KC]).then_inc(bl[rb], 16)

            sp.wait_ge(con, 2)
            w = 0
            for p in range(PR + 1):
                for i in range(len(KINDS)):
                    if p < PR:
                        if w >= 2:
                            sp.wait_ge(wls, w - 1)
                        sp.dma_start(wr[:, w % 2, :, :], a["w_na"][w]).then_inc(wld[w % 2], 16)
                        w += 1
                    if p == 0 and i in (1, 2):
                        load_bias(0, i - 1)
                    if i == 1 and p >= 2:
                        sp.wait_ge(ga, QT * (p - 1))
                        sp.dma_start(y_dram[:, p - 2, :], gg[:, p % 2, :]).then_inc(yst, 16)
                        load_bias(p - 1, 1)
                    if i == 3 and 1 <= p < PR:
                        load_bias(p, 0)
            sp.wait_ge(ga, QT * PR)
            sp.dma_start(y_dram[:, PR - 1, :], gg[:, (PR - 1) % 2, :]).then_inc(yst, 16)
            sp.wait_ge(yst, 16 * PR)

        @block.tensor
        def _(pe):
            def unit(q):
                p, i, kd, b = units[q]
                w = p * len(KINDS) + i
                t0, n = BLOCKS[b]
                pe.wait_ge(wls, w + 1)
                if q >= 2:
                    pe.wait_ge(pev, q - 1)
                project(pe, pP[q % 2][:, 0:n], whi[:, w % 2], wlo[:, w % 2], h_hi, h_lo, t0, n).then_inc(pj, 1)

            def scores(n):
                p, qt, e, rb, cb = rest(n)
                if n % UP == 0:
                    pe.wait_ge(pev, done[p, "q"])
                if n:
                    pe.wait_ge(exs, n)
                lhs = q2[:, p % 2, e, qt * P:(qt + 1) * P]
                r0 = key_row0(rb)
                pe.matmul(pA[:, 0:NW].rearrange("p (r c) -> p r c", c=KC), lhs,
                          grid(kk[:, p % 2, :])[:, r0:r0 + KR, K0C[cb]:K0C[cb] + KC], start=True, stop=True)
                pe.matmul(pB[:, 0:NC_], lhs, kk[:, p % 2, 0:CTX], start=True, stop=True).then_inc(sc, 1)

            def turn(n, vgroups):
                pe.wait_ge(pn, n + 1)
                if n:
                    pe.wait_ge(pt0, n)
                    pe.wait_ge(pt1, n)
                pe.wait_ge(vte, vgroups)
                for j in range(JW + JC):
                    bank, c = (pT0, j) if j < 4 else (pT1, j - 4)
                    x = pe.transpose(bank[:, c * P:(c + 1) * P], pm[:, n % 2, j * P:(j + 1) * P], ident[:, :])
                x.then_inc(tr, 1)

            def values(n):
                p, qt, e, rb, cb = rest(n)
                pe.wait_ge(pt0, n + 1)
                pe.wait_ge(pt1, n + 1)
                if n >= 2:
                    pe.wait_ge(ga, n // 2)
                for j in range(JW + JC):
                    x = pe.matmul(pO[e * NAD:(e + 1) * NAD, 0:P],
                                  vt[:, p % 2, win_index(rb, cb, j), e * NAD:(e + 1) * NAD],
                                  ptr[:, n % 2, j, :], start=(j == 0), stop=(j == JW + JC - 1))
                x.then_inc(pv, 1)

            def turn_values(p, gidx, turns):
                if gidx == 0:
                    pe.wait_ge(pev, done[p, "v"])
                if turns:
                    pe.wait_ge(pt0, turns)
                v = p * VG + gidx
                if v:
                    pe.wait_ge(vte, v)
                for c, j in enumerate(range(4 * gidx, min(4 * gidx + 4, WIN + JC))):
                    x = pe.transpose(pT0[:, c * P:(c + 1) * P], vv[:, j, :], ident[:, :])
                x.then_inc(vtr, 1)

            pe.wait_ge(small, 16)
            pe.wait_ge(con, 2)
            for q in range(UPP):
                unit(q)
            for gidx in range(VG):
                turn_values(0, gidx, 0)
            groups = VG
            for n in range(NU):
                p, r = divmod(n, UP)
                scores(n)
                if r in place and p + 1 < PR:
                    unit((p + 1) * UPP + place[r])
                if n:
                    turn(n - 1, groups)
                if n >= 2:
                    values(n - 2)
                if r >= VS and p + 1 < PR:
                    turn_values(p + 1, r - VS, n)
                    groups += 1
            turn(NU - 1, groups)
            values(NU - 2)
            values(NU - 1)

        @block.scalar
        def _(act):
            def split(w):
                act.wait_ge(wld[w % 2], 16 * (w // 2 + 1))
                if w >= 2:
                    p, i = divmod(w - 2, len(KINDS))
                    act.wait_ge(pj, done[p, KINDS[i]])
                act.activation(whi[:, w % 2, :, :], wr[:, w % 2, :, :], ACT.Copy).then_inc(whs, 1)

            def take(q):
                p, i, kd, b = units[q]
                w = p * len(KINDS) + i
                t0, n = BLOCKS[b]
                act.wait_ge(pj, q + 1)
                src = pP[q % 2]
                if kd == "k":
                    x = act.activation(kk[:, p % 2, t0:t0 + n], src[:, 0:n], ACT.Copy)
                elif kd == "v":
                    if b == 0 and p:
                        act.wait_ge(vtr, p * VG)
                    if b == 0:
                        x = act.activation(vv[:, WIN:WIN + JC, :], src[:, 0:n].rearrange("p (j c) -> p j c", c=P),
                                           ACT.Copy)
                    else:
                        rows = src[:, 0:n].rearrange("p (r c) -> p r c", c=GW)
                        for cw in range(CB):
                            j = cw * (GR // 4) + (b - 1) * (QR // 4)
                            x = act.activation(vv[:, j:j + QR // 4, :].rearrange("p j (r c) -> p (j r) c", c=KC),
                                               rows[:, :, K0C[cw]:K0C[cw] + KC], ACT.Copy)
                else:
                    rb = b - 1
                    view = src[:, 0:n].rearrange("p (r c q) -> p r c q", c=CB, q=QC)

                    def tiles(ap):
                        return ap[:, rb * CB * P:(rb + 1) * CB * P].rearrange("p (c r q) -> p r c q", c=CB, q=QC)
                    if kd == "q":
                        for e in range(2):
                            lo = e * NAD
                            x = act.activation(tiles(q2[lo:lo + NAD, p % 2, e, :]), view[lo:lo + NAD], ACT.Copy,
                                               scale=NAD ** -0.5)
                    else:
                        if b == 1 and p >= 2:
                            act.wait_ge(yst, 16 * (p - 1))
                        x = act.activation(tiles(gg[:, p % 2, :]), view, ACT.Copy, scale=0.5)
                x.then_inc(pev, 1)
                if b == ublocks[kd][0] and w + 1 < PR * len(KINDS):
                    split(w + 1)
                if kd == "g" and b == 2:
                    act.wait_ge(pev, q + 1)
                    if p:
                        act.wait_ge(gs, p)
                    act.activation(th[:, :], gg[:, p % 2, :], ACT.Tanh).then_inc(tnh, 1)

            def exps(n):
                act.wait_ge(nms, n + 1)
                if n >= 2:
                    act.wait_ge(tr, n - 1)
                act.activation(pm[:, n % 2, 0:NW], s[:, n % 2, :], ACT.Exp, bias=nm[:, n % 2:n % 2 + 1],
                               accum_out=lsum[:, n % 2, 0:1])
                act.activation(pm[:, n % 2, NW:NK], pB[:, 0:NC_], ACT.Exp, bias=nm[:, n % 2:n % 2 + 1],
                               accum_out=lsum[:, n % 2, 1:2]).then_inc(exs, 1)

            def keep_turned(n):
                act.wait_ge(tr, n + 1)
                if n >= 2:
                    act.wait_ge(pv, n - 1)
                act.activation(ptr[:, n % 2, 0:4, :], pT0[:, :].rearrange("p (j c) -> p j c", c=P),
                               ACT.Copy).then_inc(pt0, 1)

            def keep_values(p, gidx):
                act.wait_ge(vtr, p * VG + gidx + 1)
                j = 4 * gidx
                n = min(4, WIN + JC - j)
                act.activation(vt[:, p % 2, j:j + n, :], pT0[:, 0:n * P].rearrange("p (j c) -> p j c", c=P),
                               ACT.Copy).then_inc(vte, 1)

            split(0)
            for q in range(UPP):
                take(q)
            for gidx in range(VG):
                keep_values(0, gidx)
            for n in range(NU):
                p, r = divmod(n, UP)
                exps(n)
                if r in place and p + 1 < PR:
                    take((p + 1) * UPP + place[r])
                if n:
                    keep_turned(n - 1)
                if r >= VS and p + 1 < PR:
                    keep_values(p + 1, r - VS)
            keep_turned(NU - 1)

        @block.gpsimd
        def _(pool):
            pool.memset(q2[:, :, :, :], 0.0).then_inc(con, 1)
            pool.memset(bias[:, :, :, :, :, :], NEG).then_inc(con, 1)
            for w in range(PR * len(KINDS)):
                pool.wait_ge(whs, w + 1)
                pool.tensor_tensor(wlo[:, w % 2, :, :], wr[:, w % 2, :, :], whi[:, w % 2, :, :].bitcast(F32),
                                   ALU.subtract).then_inc(wls, 1)

        @block.vector
        def _(dve):
            def gate_silu(p):
                dve.wait_ge(tnh, p + 1)
                dve.scalar_tensor_tensor(gg[:, p % 2, :], th[:, :], 1.0, gg[:, p % 2, :], ALU.add,
                                         ALU.mult).then_inc(gs, 1)

            def maxima(n):
                p, qt, e, rb, cb = rest(n)
                dve.wait_ge(sc, n + 1)
                if n % UP == rb * UP // RB:
                    dve.wait_ge(bl[rb], 16 * 2 * QR * (p + 1))
                if n >= 2:
                    dve.wait_ge(exs, n - 1)
                dve.tensor_tensor_reduce(s[:, n % 2, :], pA[:, 0:NW], bias[:, rb, e, cb, :, :]
                                         .rearrange("p r k -> p (r k)"), 1.0, -3e38, ALU.add, ALU.max,
                                         mx[:, n % 2, 0:1]).then_inc(mxs, 1)
                dve.tensor_reduce(mx[:, n % 2, 1:2], pB[:, 0:NC_], AX_X, ALU.max).then_inc(ls, 1)
                dve.wait_ge(mxs, n + 1)
                dve.wait_ge(ls, 3 * n + 1)
                dve.tensor_scalar(nm[:, n % 2:n % 2 + 1], mx[:, n % 2, 0:1], mx[:, n % 2, 1:2], -1.0, ALU.max,
                                  ALU.mult).then_inc(nms, 1)

            def normed(n):
                dve.wait_ge(exs, n + 1)
                dve.tensor_tensor(li[:, n % 2:n % 2 + 1], lsum[:, n % 2, 0:1], lsum[:, n % 2, 1:2],
                                  ALU.add).then_inc(ls, 1)
                dve.wait_ge(ls, 3 * n + 2)
                dve.reciprocal(li[:, n % 2:n % 2 + 1], li[:, n % 2:n % 2 + 1]).then_inc(ls, 1)
                dve.wait_ge(ls, 3 * n + 3)
                dve.tensor_scalar(pm[:, n % 2, :], pm[:, n % 2, :], li[:, n % 2:n % 2 + 1], None,
                                  ALU.mult).then_inc(pn, 1)

            def keep_turned(n):
                dve.wait_ge(tr, n + 1)
                if n >= 2:
                    dve.wait_ge(pv, n - 1)
                dve.tensor_copy(ptr[:, n % 2, 4, :], pT1[:, 0:P]).then_inc(pt1, 1)

            def gated(n):
                p, qt, e, rb, cb = rest(n)
                if e == 0:
                    return
                dve.wait_ge(pv, n + 1)
                if qt == 0:
                    dve.wait_ge(gs, p + 1)
                o = gg[:, p % 2, qt * P:(qt + 1) * P]
                dve.tensor_tensor(o, pO[:, 0:P], o, ALU.mult).then_inc(ga, 1)

            gate_silu(0)
            for n in range(NU):
                p, r = divmod(n, UP)
                maxima(n)
                normed(n)
                if n:
                    keep_turned(n - 1)
                if n >= 2:
                    gated(n - 2)
                if r == UP - 1 and p + 1 < PR:
                    gate_silu(p + 1)
            keep_turned(NU - 1)
            gated(NU - 2)
            gated(NU - 1)


def program(nc, a, out, upto=None):
    stored = [nc.alloc_semaphore(f"stored{i}") for i in range(DEPTH)]
    mod_rows = nc.dram_tensor("mod_rows", [2, DEPTH, 3 * D], F32).ap()
    mod_cols = nc.dram_tensor("mod_cols", [P, DEPTH, 2 * KT, 2], F32).ap()
    tabs = nc.dram_tensor("tabs", [GROUPS, P, TABS, NCH, 2 * HPG], F32).ap()
    x1 = nc.dram_tensor("x1", [TOK, D], F32).ap()
    y1 = nc.dram_tensor("y1", [P, D // P, SEQ], F32).ap()
    pad = nc.dram_tensor("pad", [NAH * DR, PADW], F32).ap()
    bt = nc.dram_tensor("bt", [CB * QC, NAH * DR, KC], F32).ap()
    y0 = nc.dram_tensor("y0", [P, YT, TOK], F32).ap()

    def x0(t):
        return a["ctx"][t * P:(t + 1) * P, :] if t < CCH else a["x"][(t - CCH) * P:(t - CCH + 1) * P, :]

    modulation(nc, a, mod_rows, mod_cols)
    bias_tables(nc, a, pad, bt)
    with ExitStack() as ctx:
        m = Mem(nc, ctx, "h0")
        h_hi = m.sb("h_hi", [P, KT, TOK], F32R)
        h_lo = m.sb("h_lo", [P, KT, TOK], F32R)
        norm_transpose(nc, a, 0, x0, mod_cols, mod_rows, h_hi, h_lo)
        time_steps(nc, a, h_hi, h_lo, tabs)
        ssd_groups(nc, a, h_hi, h_lo, tabs, y0)

    def rows(ap, t):
        return ap[t * P:(t + 1) * P, :]

    out_project(nc, a, 0, y0, YT, a["w_ssd_out"],
                [(t * P, t < CCH, lambda b, t=t: (b, x0(t)), lambda b, t=t: (rows(x1, t), b)) for t in range(NCH)],
                mod_rows, stored[0])
    with ExitStack() as ctx:
        m = Mem(nc, ctx, "h1")
        h_hi = m.sb("h_hi", [P, KT, TOK], F32R)
        h_lo = m.sb("h_lo", [P, KT, TOK], F32R)
        norm_transpose(nc, a, 1, lambda t: rows(x1, t), mod_cols, mod_rows, h_hi, h_lo)
        attention(nc, a, h_hi, h_lo, bt, y1)

    def patch(ap, t):
        rb, cb = divmod(t, CB)
        return ap.rearrange("(r c) d -> r c d", c=GW)[rb * QR:(rb + 1) * QR, cb * QC:(cb + 1) * QC, :]

    out_project(nc, a, 1, y1, D // P, a["w_na_out"],
                [(t * P, False, lambda b, t=t: (b, patch(x1[CTX:TOK, :], t)), lambda b, t=t: (patch(out, t), b))
                 for t in range(SEQ // P)], mod_rows, stored[1])
    return dict(mod_rows=mod_rows, mod_cols=mod_cols, tabs=tabs, y0=y0)


def column_mask():
    qcol = np.arange(GW).reshape(CB, QC, 1)
    start = np.clip(qcol - WC // 2, 0, GW - WC)
    kcol = np.array(K0C).reshape(CB, 1, 1) + np.arange(KC)
    return np.where((kcol >= start) & (kcol < start + WC), 0.0, NEG).astype(np.float32).reshape(CB * QC, KC)


def lay_out(x, c, ctx, c_ctx, ada_w, ada_b, pre_g, post_g, ssd_w_in, ssd_conv_w, ssd_conv_b, ssd_dt_bias,
            ssd_a_log, ssd_d, ssd_norm_g, ssd_w_out, na_w_in, na_rpb, na_w_out):
    asc = np.ascontiguousarray
    f32 = np.float32
    w = np.asarray(ssd_w_in)[0]
    gn = GROUPS * NST

    def tile(cols):
        return w[:, cols:cols + P].reshape(KT, P, P).transpose(1, 0, 2)

    def xtile(g, i):
        return DI + ((2 * g + i) * P if i < 2 else DI + (g * P if i == 2 else gn + g * P))

    order = [xtile(0, i) for i in range(4)]
    for g in range(GROUPS):
        nxt = [xtile(g + 1, i) for i in range(4)] if g + 1 < GROUPS else []
        order += nxt[:1] + [(2 * g) * P, (2 * g + 1) * P] + nxt[1:]
    conv = np.concatenate([np.asarray(ssd_conv_w)[0], np.asarray(ssd_conv_b)], axis=0)
    cv = np.stack([np.stack([conv[:, xtile(g, i) - DI:xtile(g, i) - DI + P].T for i in range(4)], 1)
                   for g in range(GROUPS)], 1)
    wdt = np.concatenate([w[:, 2 * DI + 2 * gn:], np.zeros((D, P - 2 * HEADS), w.dtype)], axis=1)
    tri = np.tril(np.ones((P, P), f32))
    a = {
        "x": np.asarray(x)[0], "ctx": np.asarray(ctx)[0],
        "cvec": np.stack([np.asarray(c)[0], np.asarray(c_ctx)], 1).reshape(KT, P, 2).transpose(1, 0, 2),
        "ada_w": ada_w, "ada_b": ada_b,
        "pre_g": np.asarray(pre_g).reshape(DEPTH, KT, P).transpose(0, 2, 1), "post_g": post_g,
        "w_ssd": np.stack([tile(o) for o in order]), "w_dt": wdt.reshape(KT, P, P).transpose(1, 0, 2),
        "conv": cv, "dt_bias": np.asarray(ssd_dt_bias)[0].reshape(-1), "a_log": np.asarray(ssd_a_log)[0].reshape(-1),
        "dskip": np.repeat(np.asarray(ssd_d)[0], HD), "norm_g": np.asarray(ssd_norm_g)[0].reshape(YT, P).T,
        "w_ssd_out": np.asarray(ssd_w_out)[0], "w_na_out": np.asarray(na_w_out)[0],
        "w_na": np.stack([np.asarray(na_w_in)[0][:, o + p * P:o + (p + 1) * P].reshape(KT, P, P).transpose(1, 0, 2)
                          for p in range(NAH // 2) for o in (2 * D, D, 0, 3 * D)]),
        "rpb": np.asarray(na_rpb)[0].reshape(NAH * DR, DC), "colmask": column_mask(),
        "ident": np.eye(P, dtype=f32), "m_le": asc(tri.T), "m_ge": tri,
    }
    return {n: asc(v) for n, v in a.items()}


def kernel(**inputs):
    from concourse import bacc
    from concourse.bass_utils import run_bass_kernel_spmd

    arrays = lay_out(**inputs)
    nc = bacc.Bacc("TRN2", target_bir_lowering=False, num_devices=1)
    a = {n: nc.dram_tensor(f"in_{n}", v.shape, mybir.dt.from_np(v.dtype), kind="ExternalInput").ap()
         for n, v in arrays.items()}
    out = nc.dram_tensor("out", (SEQ, D), F32, kind="ExternalOutput").ap()
    program(nc, a, out)
    r = run_bass_kernel_spmd(nc, [{f"in_{n}": v for n, v in arrays.items()}], core_ids=[0])
    return r.results[0]["out"].reshape(1, SEQ, D)
```

```python
from contextlib import ExitStack

import concourse.bass as bass
import numpy as np
from concourse import mybir

F32 = mybir.dt.float32
F32R = mybir.dt.float32r
ACT = mybir.ActivationFunctionType
ALU = mybir.AluOpType
AX_X = mybir.AxisListType.X

P = 128
D = 1024
KT = D // P
SEQ, CTX = 1024, 256
TOK = SEQ + CTX
NCH = TOK // P
CCH = CTX // P
DEPTH = 2
GROUPS, HPG, HD, NST = 8, 4, 64, 128
HEADS = GROUPS * HPG
DI = HEADS * HD
YT = DI // P
EPS = 1e-6
BLOCKS = ((0, 256), (256, 512), (768, 512))
NBL = len(BLOCKS)

UW = TOK + 4
TABS = 6
A_HI, A_LO, DT, DTDEC, ECUM, ETOT = range(TABS)


def ucol(t):
    return t + 1 if t < CTX else t + 3


class Mem:

    def __init__(self, nc, ctx, tag):
        self.nc, self.ctx, self.tag, self.sems = nc, ctx, tag, []
        ctx.callback(self.release)

    def release(self):
        if self.sems:
            self.nc.clear_and_free_semaphores(self.sems)
            self.nc.all_engine_barrier()

    def sb(self, name, shape, dt=F32):
        return self.ctx.enter_context(self.nc.sbuf_tensor(f"{self.tag}_{name}", shape, dt))

    def ps(self, name, dt=F32, n=512):
        return self.ctx.enter_context(self.nc.psum_tensor(f"{self.tag}_{name}", [P, n], dt))

    def sem(self, name):
        self.sems.append(self.nc.alloc_semaphore(f"{self.tag}_{name}"))
        return self.sems[-1]


NRUN0, NRUN1 = 18, 38


class Modulation:
    NC = 512
    KC4 = NC // P

    def __init__(self, nc, m, a, csil, chunks, ring, mod_rows, mod_cols):
        self.a, self.csil, self.chunks, self.ring = a, csil, chunks, ring
        self.mod_rows, self.mod_cols = mod_rows, mod_cols
        n = len(chunks)
        self.w = m.sb("mod_w", [P, ring, KT, self.NC])
        self.bias = m.sb("mod_bias", [2, n, self.NC])
        self.rows = m.sb("mod_rows", [2, n, self.NC])
        self.cols = m.sb("mod_cols", [P, n, self.KC4, 2])
        self.ident = m.sb("mod_ident", [2, 2])
        self.pacc = [m.ps(f"mod_pacc{i}") for i in range(2)]
        self.pcol = m.ps("mod_pcol")
        self.acc, self.evac, self.turned, self.kept, self.stored = map(m.sem, (
            "mod_acc", "mod_evac", "mod_turned", "mod_kept", "mod_stored"))
        self.wld = [m.sem(f"mod_wld{i}") for i in range(ring)]
        self.small = m.sem("mod_small")

    def turns(self, n):
        return sum(c < 4 for _, c in self.chunks[:n])

    def load_small(self, sp):
        sp.dma_start(self.ident[:, :], self.a["ident"][0:2, 0:2]).then_inc(self.small, 16)
        for n, (i, c) in enumerate(self.chunks):
            sp.dma_start(self.bias[:, n, :], self.a["ada_b"][i, c * self.NC:(c + 1) * self.NC]
                         .partition_broadcast(2)).then_inc(self.small, 16)

    def load(self, sp, n):
        i, c = self.chunks[n]
        if n >= self.ring:
            sp.wait_ge(self.acc, n - self.ring + 1)
        sp.dma_start(self.w[:, n % self.ring, :, :],
                     self.a["ada_w"][i].rearrange("(k p) n -> p k n", p=P)[:, :, c * self.NC:(c + 1) * self.NC]
                     ).then_inc(self.wld[n % self.ring], 16)

    def products(self, pe, n, ks=range(KT)):
        if ks[0] == 0:
            pe.wait_ge(self.wld[n % self.ring], 16 * (n // self.ring + 1))
            if n >= 2:
                pe.wait_ge(self.evac, n - 1)
        for k in ks:
            x = pe.matmul(self.pacc[n % 2][0:2, :], self.csil[:, k, :], self.w[:, n % self.ring, k, :],
                          start=(k == 0), stop=(k == KT - 1))
        if ks[-1] == KT - 1:
            x.then_inc(self.acc, 1)

    def turn(self, pe, n):
        if self.chunks[n][1] >= 4:
            return
        pe.wait_ge(self.small, 16 * (1 + len(self.chunks)))
        pe.wait_ge(self.evac, n + 1)
        if self.turns(n):
            pe.wait_ge(self.kept, self.turns(n))
        for k in range(self.KC4):
            x = pe.transpose(self.pcol[:, 2 * k:2 * k + 2], self.rows[:, n, k * P:(k + 1) * P], self.ident[:, :])
        x.then_inc(self.turned, 1)

    def add_bias(self, dve, n):
        if n == 0:
            dve.wait_ge(self.small, 16 * (1 + len(self.chunks)))
        dve.wait_ge(self.acc, n + 1)
        dve.tensor_tensor(self.rows[:, n, :], self.pacc[n % 2][0:2, :], self.bias[:, n, :],
                          ALU.add).then_inc(self.evac, 1)

    def keep(self, dve, n):
        if self.chunks[n][1] >= 4:
            return
        dve.wait_ge(self.turned, self.turns(n) + 1)
        dve.tensor_copy(self.cols[:, n, :, :], self.pcol[:, 0:2 * self.KC4].rearrange("p (k v) -> p k v", v=2)
                        ).then_inc(self.kept, 1)

    def store(self, sp):
        for n, (i, c) in enumerate(self.chunks):
            if c < 4:
                sp.wait_ge(self.kept, self.turns(n) + 1)
                sp.dma_start(self.mod_cols[:, i, c * self.KC4:(c + 1) * self.KC4, :],
                             self.cols[:, n, :, :]).then_inc(self.stored, 16)
            else:
                sp.wait_ge(self.evac, n + 1)
                sp.dma_start(self.mod_rows[:, i, c * self.NC:(c + 1) * self.NC],
                             self.rows[:, n, :]).then_inc(self.stored, 16)
        sp.wait_ge(self.stored, 16 * len(self.chunks))


def gather_runs(q, pad_dram, run_dram, which, done):
    for cq in which:
        c, qc = divmod(cq, QC)
        first = QC + WC - 1 + K0C[c] - QC * c - qc
        q.dma_start(run_dram[cq, :, :], pad_dram[:, first:first + KC]).then_inc(done, 16)


def first_modulation(nc, a, csil, chunks, mod_rows, mod_cols, pad_dram, run_dram):
    NR = NAH * DR
    N = len(chunks)
    with ExitStack() as ctx:
        m = Mem(nc, ctx, "md")
        craw = m.sb("craw", [P, KT, 2])
        cth = m.sb("cth", [P, KT, 2])
        prow = [m.sb(f"prow{i}", [NR // 2, PADW]) for i in range(2)]
        small, sil, zeroed, rld, pd, run = map(m.sem, ("small", "sil", "zeroed", "rld", "pd", "run"))
        mod = Modulation(nc, m, a, csil, chunks, N, mod_rows, mod_cols)
        block = ctx.enter_context(nc.Block())

        @block.sync
        def _(sp):
            sp.dma_start(craw[:, :, :], a["cvec"]).then_inc(small, 16)
            mod.load(sp, 0)
            mod.load(sp, 1)
            mod.load_small(sp)
            for n in range(2, N):
                mod.load(sp, n)
            sp.wait_ge(zeroed, 2)
            for i in range(2):
                sp.dma_start(prow[i][:, QC:QC + DC], a["rpb"][i * NR // 2:(i + 1) * NR // 2, :]).then_inc(rld, 16)
            sp.wait_ge(rld, 32)
            for i in range(2):
                sp.dma_start(pad_dram[i * NR // 2:(i + 1) * NR // 2, :], prow[i][:, :]).then_inc(pd, 16)
            sp.wait_ge(pd, 32)
            gather_runs(sp, pad_dram, run_dram, range(NRUN0), run)
            mod.store(sp)
            sp.wait_ge(run, 16 * NRUN0)

        @block.scalar
        def _(act):
            act.wait_ge(small, 16)
            act.activation(cth[:, :, :], craw[:, :, :], ACT.Tanh, scale=0.5).then_inc(sil, 1)

        @block.vector
        def _(dve):
            for i in range(2):
                dve.memset(prow[i][:, :], 0.0).then_inc(zeroed, 1)
            dve.wait_ge(sil, 1)
            dve.scalar_tensor_tensor(csil[:, :, :], cth[:, :, :], 1.0, craw[:, :, :],
                                     ALU.add, ALU.mult).then_inc(sil, 1)
            dve.wait_ge(sil, 2)
            dve.tensor_scalar(csil[:, :, :], csil[:, :, :], 0.5, None, ALU.mult).then_inc(sil, 1)
            for n in range(N):
                mod.add_bias(dve, n)
                if n:
                    mod.keep(dve, n - 1)
            mod.keep(dve, N - 1)

        @block.tensor
        def _(pe):
            pe.wait_ge(sil, 3)
            for n in range(N):
                mod.products(pe, n)
                if n:
                    mod.turn(pe, n - 1)
            mod.turn(pe, N - 1)


def norm_transpose(nc, a, layer, x_in, mod_cols, mod_rows, h_hi, h_lo, csil=None, chunks=(), pad_dram=None, run_dram=None):
    R = 4
    KA = 4
    N = len(chunks)
    steps_after = [[j for j in range(N * KT) if 1 + j * (NCH - 1) // (N * KT) == t] for t in range(NCH)]
    ends_after = [[j // KT for j in steps if j % KT == KT - 1] for steps in steps_after]
    with ExitStack() as ctx:
        m = Mem(nc, ctx, f"nt{layer}")
        x = m.sb("x", [P, R, D])
        sq = m.sb("sq", [P, D])
        st = m.sb("st", [P, NCH])
        var = m.sb("var", [P, NCH])
        rstd = m.sb("rstd", [P, NCH])
        mhalf = m.sb("mhalf", [P, 1])
        xn = m.sb("xn", [P, 2, D])
        h32 = m.sb("h32", [P, 2, KT, P])
        preg = m.sb("preg", [P, KT])
        mc = m.sb("mc", [P, 2 * KT, 2])
        gain = m.sb("gain", [P, KT, 2])
        ident = m.sb("ident", [P, P])
        pt = [m.ps(f"pt{i}") for i in range(4)]
        small, con, gn, ssq, vr, rs, nrm, tr, h3, h3d, hi, hia, lo = map(
            m.sem, ("small", "con", "gn", "ssq", "vr", "rs", "nrm", "tr", "h3", "h3d", "hi", "hia", "lo"))
        ld = [m.sem(f"ld{i}") for i in range(R)]
        mod = Modulation(nc, m, a, csil, chunks, N, mod_rows, mod_cols) if N else None
        run = m.sem("run")
        runs = range(NRUN0, NRUN1)
        block = ctx.enter_context(nc.Block())

        @block.sync
        def _(sp):
            for t in range(NCH):
                if t >= R:
                    sp.wait_ge(nrm, t - R + 1)
                sp.dma_start(x[:, t % R, :], x_in(t)).then_inc(ld[t % R], 16)
                if t == 0:
                    sp.dma_start(preg[:, :], a["pre_g"][layer]).then_inc(small, 16)
                    sp.dma_start(mc[:, :, :], mod_cols[:, layer, :, :]).then_inc(small, 16)
                    sp.dma_start(ident[:, :], a["ident"]).then_inc(small, 16)
                if t == R - 1 and N:
                    mod.load_small(sp)
                if t % 2 and t // 2 < N:
                    mod.load(sp, t // 2)
                if pad_dram is not None and t >= R - 1:
                    k = t - R + 1
                    gather_runs(sp, pad_dram, run_dram, runs[k::NCH - R + 1], run)
            if N:
                mod.store(sp)
            if pad_dram is not None:
                sp.wait_ge(run, 16 * len(runs))

        @block.scalar
        def _(act):
            def square(t):
                act.wait_ge(ld[t % R], 16 * (t // R + 1))
                if t:
                    act.wait_ge(ssq, t)
                act.activation(sq[:, :], x[:, t % R, :], ACT.Square, accum_out=st[:, t:t + 1]).then_inc(ssq, 1)

            square(0)
            square(1)
            act.wait_ge(gn, 2)
            for t in range(NCH):
                if t + 2 < NCH:
                    square(t + 2)
                v = 1 if t < CCH else 0
                act.wait_ge(tr, t + 1)
                if t >= 2:
                    act.wait_ge(lo, t - 1)
                for k in range(KA):
                    y = act.activation(h32[:, t % 2, k, :], pt[2 * (t % 2) + k // 4][:, (k % 4) * P:(k % 4 + 1) * P],
                                       ACT.Identity, bias=mc[:, k, v:v + 1], scale=gain[:, k, v:v + 1])
                y.then_inc(h3, 1)
                act.wait_ge(h3, t + 1)
                act.activation(h_hi[:, 0:KA, t * P:(t + 1) * P], h32[:, t % 2, 0:KA, :], ACT.Copy).then_inc(hia, 1)

        @block.gpsimd
        def _(pool):
            pool.memset(mhalf[:, :], -0.5).then_inc(con, 1)
            pool.wait_ge(con, 1)
            for t in range(NCH):
                pool.wait_ge(vr, t + 1)
                pool.tensor_tensor(rstd[:, t:t + 1], var[:, t:t + 1], mhalf[:, :], ALU.pow).then_inc(rs, 1)

        @block.vector
        def _(dve):
            def variance(t):
                dve.wait_ge(ssq, t + 1)
                dve.tensor_scalar(var[:, t:t + 1], st[:, t:t + 1], 1.0 / D, EPS, ALU.mult, ALU.add).then_inc(vr, 1)

            def norm(t):
                dve.wait_ge(rs, t + 1)
                if t >= 2:
                    dve.wait_ge(tr, t - 1)
                dve.tensor_scalar(xn[:, t % 2, :], x[:, t % R, :], rstd[:, t:t + 1], None, ALU.mult).then_inc(nrm, 1)

            variance(0)
            variance(1)
            norm(0)
            dve.wait_ge(small, 48)
            dve.tensor_scalar(gain[:, :, :], mc[:, KT:2 * KT, :], 1.0, None, ALU.add).then_inc(gn, 1)
            dve.wait_ge(gn, 1)
            dve.tensor_tensor(gain[:, :, :], gain[:, :, :], preg[:, :].unsqueeze(2).to_broadcast([P, KT, 2]),
                              ALU.mult).then_inc(gn, 1)
            for t in range(NCH):
                if t + 2 < NCH:
                    variance(t + 2)
                if t + 1 < NCH:
                    norm(t + 1)
                v = 1 if t < CCH else 0
                dve.wait_ge(tr, t + 1)
                if t >= 2:
                    dve.wait_ge(lo, t - 1)
                for k in range(KA, KT):
                    y = dve.tensor_scalar(h32[:, t % 2, k, :],
                                          pt[2 * (t % 2) + k // 4][:, (k % 4) * P:(k % 4 + 1) * P],
                                          gain[:, k, v:v + 1], mc[:, k, v:v + 1], ALU.mult, ALU.add)
                y.then_inc(h3d, 1)
                dve.wait_ge(h3d, t + 1)
                dve.tensor_copy(h_hi[:, KA:KT, t * P:(t + 1) * P], h32[:, t % 2, KA:KT, :]).then_inc(hi, 1)
                dve.wait_ge(hi, t + 1)
                dve.wait_ge(hia, t + 1)
                dve.tensor_tensor(h_lo[:, :, t * P:(t + 1) * P], h32[:, t % 2, :, :],
                                  h_hi[:, :, t * P:(t + 1) * P].bitcast(F32), ALU.subtract).then_inc(lo, 1)
                for n in ends_after[t - 1] if t else ():
                    mod.add_bias(dve, n)
                for n in ends_after[t - 2] if t > 1 else ():
                    mod.keep(dve, n)
            for n in ends_after[NCH - 2]:
                mod.keep(dve, n)
            for n in ends_after[NCH - 1]:
                mod.add_bias(dve, n)
                mod.keep(dve, n)

        @block.tensor
        def _(pe):
            pe.wait_ge(small, 48)
            for t in range(NCH):
                pe.wait_ge(nrm, t + 1)
                if t >= 2:
                    pe.wait_ge(h3, t - 1)
                    pe.wait_ge(h3d, t - 1)
                for k in range(KT):
                    y = pe.transpose(pt[2 * (t % 2) + k // 4][:, (k % 4) * P:(k % 4 + 1) * P],
                                     xn[:, t % 2, k * P:(k + 1) * P], ident[:, :])
                y.then_inc(tr, 1)
                for n in sorted({j // KT for j in steps_after[t]}):
                    mod.products(pe, n, [j % KT for j in steps_after[t] if j // KT == n])
                for n in ends_after[t - 1] if t else ():
                    mod.turn(pe, n)
            for n in ends_after[NCH - 1]:
                mod.turn(pe, n)


def time_steps(nc, a, h_hi, h_lo, tabs_dram, csil, chunks, mod_rows, mod_cols, pad_dram, run_dram, bt_dram):
    H2 = 2 * HEADS
    NR = NAH * DR
    N = len(chunks)
    with ExitStack() as ctx:
        m = Mem(nc, ctx, "ts")
        wr = m.sb("wr", [P, KT, P])
        whi = m.sb("whi", [P, KT, P], F32R)
        wlo = m.sb("wlo", [P, KT, P], F32R)
        raw = m.sb("raw", [P, TOK])
        full = lambda name, dt=F32: m.sb(name, [P, NCH, H2], dt)
        v, e, s, q, dt, av, cum, etot = map(full, ("v", "e", "s", "q", "dt", "av", "cum", "etot"))
        ahr = full("ahr", F32R)
        ecum, dec, dtdec, alo = v, e, s, q
        out = m.sb("out", [P, GROUPS, TABS, NCH, 2 * HPG])
        bias = m.sb("bias", [P, H2])
        alog = m.sb("alog", [P, H2])
        ident, le, ge, ones = (m.sb(n, [P, P]) for n in ("ident", "le", "ge", "ones"))
        pp = [m.ps(f"pp{i}") for i in range(NBL)]
        pT = [m.ps(f"pT{i}") for i in range(2)]
        pc = pp[0:2]
        NQ = CB * QC
        T = m.sb("T", [2 * NQ, NR // 2, KC])
        mask = m.sb("mask", [2 * NQ, KC])
        small, split, pr, rw, tr, vv, ch, ex, cm, tot, pk, st = map(
            m.sem, ("small", "split", "pr", "rw", "tr", "vv", "ch", "ex", "cm", "tot", "pk", "st"))
        run, wn, ad, bst = map(m.sem, ("run", "wn", "ad", "bst"))
        mod = Modulation(nc, m, a, csil, chunks, 2, mod_rows, mod_cols)
        block = ctx.enter_context(nc.Block())
        HALF = NCH // 2

        @block.sync
        def _(sp):
            sp.dma_start(wr[:, :, :], a["w_dt"]).then_inc(small, 16)
            sp.dma_start(bias[:, :], a["dt_bias"].partition_broadcast(P)).then_inc(small, 16)
            sp.dma_start(alog[:, :], a["a_log"].partition_broadcast(P)).then_inc(small, 16)
            sp.dma_start(ident[:, :], a["ident"]).then_inc(small, 16)
            sp.dma_start(le[:, :], a["m_le"]).then_inc(small, 16)
            sp.dma_start(ge[:, :], a["m_ge"]).then_inc(small, 16)
            mod.load(sp, 0)
            mod.load(sp, 1)
            mod.load_small(sp)
            for half in range(2):
                sp.dma_start(mask[half * NQ:(half + 1) * NQ, :], a["colmask"]).then_inc(wn, 16)
            gather_runs(sp, pad_dram, run_dram, range(NRUN1, NQ), run)
            sp.wait_ge(run, 16 * (NQ - NRUN1))
            for half in range(2):
                sp.dma_start(T[half * NQ:(half + 1) * NQ, :, :],
                             run_dram[:, half * NR // 2:(half + 1) * NR // 2, :]).then_inc(wn, 16)
            for n in range(2, N):
                mod.load(sp, n)
            sp.wait_ge(ad, 1)
            for half in range(2):
                sp.dma_start(bt_dram[:, half * NR // 2:(half + 1) * NR // 2, :],
                             T[half * NQ:(half + 1) * NQ, :, :]).then_inc(bst, 16)
            sp.wait_ge(pk, 1)
            sp.dma_start(tabs_dram.rearrange("g p t c h -> p g t c h"), out[:, :, :, :, :]).then_inc(st, 16)
            mod.store(sp)
            sp.wait_ge(st, 16)
            sp.wait_ge(bst, 32)

        @block.gpsimd
        def _(pool):
            pool.memset(ones[:, :], 1.0).then_inc(small, 1)
            pool.wait_ge(wn, 64)
            pool.tensor_tensor(T[:, :, :], T[:, :, :], mask[:, :].unsqueeze(1).to_broadcast([2 * NQ, NR // 2, KC]),
                               ALU.add).then_inc(ad, 1)

        @block.scalar
        def _(act):
            act.wait_ge(small, 97)
            act.activation(whi[:, :, :], wr[:, :, :], ACT.Copy).then_inc(split, 1)
            for b, (t0, n) in enumerate(BLOCKS):
                act.wait_ge(pr, b + 1)
                act.activation(raw[:, t0:t0 + n], pp[b][:, 0:n], ACT.Copy).then_inc(rw, 1)
            act.wait_ge(vv, 1)
            act.activation(e[:, :, :], v[:, :, :], ACT.Abs).then_inc(ex, 1)
            act.wait_ge(ex, 1)
            act.activation(e[:, :, :], e[:, :, :], ACT.Exp, scale=-1.0).then_inc(ex, 1)
            act.activation(alog[:, :], alog[:, :], ACT.Exp).then_inc(ex, 1)
            act.wait_ge(cm, 2)
            for i in range(2):
                act.activation(cum[:, :, i * HEADS:(i + 1) * HEADS],
                               pc[i][:, 0:NCH * HEADS].rearrange("p (c h) -> p c h", c=NCH),
                               ACT.Copy).then_inc(ex, 1)
            act.wait_ge(ex, 5)
            act.activation(ecum[:, :, :], cum[:, :, :], ACT.Exp).then_inc(ex, 1)
            act.wait_ge(tot, 2)
            for i in range(2):
                act.activation(etot[:, i * HALF:(i + 1) * HALF, :],
                               pT[i][:, 0:HALF * H2].rearrange("p (c h) -> p c h", h=H2), ACT.Copy).then_inc(ex, 1)
            act.wait_ge(ch, 19)
            act.activation(dec[:, :, :], dec[:, :, :], ACT.Exp).then_inc(ex, 1)
            act.activation(etot[:, :, :], etot[:, :, :], ACT.Exp).then_inc(ex, 1)

        @block.vector
        def _(dve):
            dve.wait_ge(split, 1)
            dve.tensor_tensor(wlo[:, :, :], wr[:, :, :], whi[:, :, :].bitcast(F32), ALU.subtract).then_inc(split, 1)
            dve.wait_ge(tr, 2)
            n = [0]

            def step(x):
                x.then_inc(ch, 1)
                n[0] += 1
                dve.wait_ge(ch, n[0])

            for i in range(2):
                x = dve.tensor_tensor(v[:, i * HALF:(i + 1) * HALF, :],
                                      pT[i][:, 0:HALF * H2].rearrange("p (c h) -> p c h", h=H2),
                                      bias[:, :].unsqueeze(1).to_broadcast([P, HALF, H2]), ALU.add)
            x.then_inc(vv, 1)
            dve.wait_ge(ex, 2)
            step(dve.tensor_scalar(s[:, :, :], e[:, :, :], 2.0, None, ALU.add))
            step(dve.reciprocal(q[:, :, :], s[:, :, :]))
            mod.add_bias(dve, 0)
            step(dve.tensor_tensor(s[:, :, :], q[:, :, :], e[:, :, :], ALU.mult))
            step(dve.tensor_tensor(dt[:, :, :], s[:, :, :], s[:, :, :], ALU.mult))
            step(dve.tensor_scalar(q[:, :, :], dt[:, :, :], 1.0 / 17, None, ALU.mult))
            for k in range(15, 1, -2):
                step(dve.scalar_tensor_tensor(q[:, :, :], q[:, :, :], 1.0 / k, dt[:, :, :], ALU.add, ALU.mult))
            step(dve.scalar_tensor_tensor(q[:, :, :], q[:, :, :], 1.0, s[:, :, :], ALU.add, ALU.mult))
            step(dve.tensor_scalar(v[:, :, :], v[:, :, :], 0.0, None, ALU.max))
            step(dve.scalar_tensor_tensor(dt[:, :, :], q[:, :, :], 2.0, v[:, :, :], ALU.mult, ALU.add))
            dve.wait_ge(ex, 3)
            step(dve.scalar_tensor_tensor(av[:, :, :], dt[:, :, :], -1.0,
                                          alog[:, :].unsqueeze(1).to_broadcast([P, NCH, H2]), ALU.mult, ALU.mult))
            step(dve.tensor_copy(ahr[:, :, :], av[:, :, :]))
            step(dve.tensor_tensor(alo[:, :, :], av[:, :, :], ahr[:, :, :].bitcast(F32), ALU.subtract))
            assert n[0] == 18
            mod.add_bias(dve, 1)
            dve.wait_ge(ex, 8)
            step(dve.tensor_tensor(dec[:, :, :], etot[:, :, :], cum[:, :, :], ALU.subtract))
            dve.wait_ge(ex, 10)
            step(dve.tensor_tensor(dtdec[:, :, :], dt[:, :, :], dec[:, :, :], ALU.mult))
            for i, t in enumerate((ahr[:, :, :].bitcast(F32), alo, dt, dtdec, ecum, etot)):
                for d in range(2):
                    x = dve.tensor_copy(out[:, :, i, :, d * HPG:(d + 1) * HPG],
                                        t[:, :, d * HEADS:(d + 1) * HEADS].rearrange("p c (g h) -> p g c h", h=HPG))
            x.then_inc(pk, 1)
            mod.add_bias(dve, 2)
            for n in range(3, N):
                mod.add_bias(dve, n)
            for n in range(N):
                mod.keep(dve, n)

        @block.tensor
        def _(pe):
            pe.wait_ge(split, 2)
            for b, (t0, n) in enumerate(BLOCKS):
                x = project(pe, pp[b][:, 0:n], whi, wlo, h_hi, h_lo, t0, n)
                x.then_inc(pr, 1)
            pe.wait_ge(rw, NBL)
            for c in range(NCH):
                x = pe.transpose(pT[c // HALF][:, (c % HALF) * H2:(c % HALF + 1) * H2],
                                 raw[0:H2, c * P:(c + 1) * P], ident[0:H2, 0:H2])
                if c % HALF == HALF - 1:
                    x.then_inc(tr, 1)
            mod.products(pe, 0)
            mod.products(pe, 1)
            mod.products(pe, 2)
            pe.wait_ge(ch, 16)
            for i, tri in enumerate((le, ge)):
                pe.matmul(pc[i][:, 0:NCH * HEADS], tri[:, :], av[:, :, i * HEADS:(i + 1) * HEADS],
                          start=True, stop=True).then_inc(cm, 1)
            for i in range(2):
                pe.matmul(pT[i][:, 0:HALF * H2], ones[:, :], av[:, i * HALF:(i + 1) * HALF, :],
                          start=True, stop=True).then_inc(tot, 1)
            for n in range(3, N):
                mod.products(pe, n)
            for n in range(N):
                mod.turn(pe, n)


def project(pe, out, w_hi, w_lo, h_hi, h_lo, t0, n, ks=range(KT)):
    for k in ks:
        pe.matmul(out, w_hi[:, k, :], h_hi[:, k, t0:t0 + n], start=(k == 0), stop=False)
        pe.matmul(out, w_hi[:, k, :], h_lo[:, k, t0:t0 + n], start=False, stop=False)
        x = pe.matmul(out, w_lo[:, k, :], h_hi[:, k, t0:t0 + n], start=False, stop=(k == KT - 1))
    return x


def ssd_groups(nc, a, h_hi, h_lo, tabs_dram, y_dram):
    UN = DI // GROUPS
    PAIRS = UN // P
    XT = PAIRS + 2
    B_, C_ = PAIRS, PAIRS + 1
    G = GROUPS
    BACK = list(range(CCH - 1, -1, -1)) + list(range(NCH - 1, CCH - 1, -1))
    H8 = 2 * HPG
    SLOTS = 2 * NCH

    tiles = [("x", 0, i) for i in range(XT)]
    for g in range(G):
        z = [("z", g, i) for i in range(PAIRS)]
        x = [("x", g + 1, i) for i in range(XT)] if g + 1 < G else []
        tiles += x[:1] + z + x[1:]
    w_of = {t: w for w, t in enumerate(tiles)}
    PRO = NBL * XT
    per = NBL * (XT + PAIRS)
    z_slots = list(range(NCH - NBL * PAIRS, NCH))
    slots_of = {g: (list(range(NBL)) if g + 1 < G else []) + z_slots +
                (list(range(NCH, NCH + NBL * (XT - 1))) if g + 1 < G else []) for g in range(G)}
    line = list(range(PRO)) + [PRO + g * per + slots_of[g].index(s) if s in slots_of[g] else None
                               for g in range(G) for s in range(SLOTS)]
    units = {g: line[PRO + g * SLOTS:PRO + (g + 1) * SLOTS] for g in range(G)}
    x_unit = lambda g, b: NBL * w_of[("x", g, XT - 1)] + b
    z_unit = lambda g, b: NBL * w_of[("z", g, PAIRS - 1)] + b
    x_before = [0]
    for q in range(NBL * len(tiles)):
        x_before.append(x_before[-1] + (tiles[q // NBL][0] == "x"))
    SPAN = ((ucol(0), ucol(CTX - 1) + 1), (ucol(CTX), ucol(BLOCKS[2][0] - 1)),
            (ucol(BLOCKS[2][0] - 1), ucol(TOK - 1) + 1))
    WIDEST = max(hi - lo for lo, hi in SPAN)
    CHUNKS = [(t0 // P, (t0 + n) // P) for t0, n in BLOCKS]
    block_of = [b for b, (lo, hi) in enumerate(CHUNKS) for _ in range(lo, hi)]

    with ExitStack() as ctx:
        m = Mem(nc, ctx, "sg")
        wr = m.sb("wr", [P, KT, P])
        whi = m.sb("whi", [P, 2, KT, P], F32R)
        wlo = m.sb("wlo", [P, 2, KT, P], F32R)
        u = m.sb("u", [P, UW])
        th = m.sb("th", [P, WIDEST])
        X = m.sb("X", [P, 2, XT, UW])
        Z = m.sb("Z", [P, PAIRS, TOK])
        tab = m.sb("tab", [P, 2, TABS, NCH, H8])
        hb = m.sb("hb", [P, NCH, UN])
        hf = m.sb("hf", [P, UN])
        cb = m.sb("cb", [P, NCH, P])
        cbm = m.sb("cbm", [P, P])
        hz = hb[:, CCH - 1, :]
        var = m.sb("var", [P, 1])
        rstd = m.sb("rstd", [P, 1])
        mhalf = m.sb("mhalf", [P, 1])
        diag = m.sb("diag", [P, P])
        aUh = m.sb("aUh", [P, H8, P], F32R)
        aUl = m.sb("aUl", [P, H8, P], F32R)
        E = m.sb("E", [P, 2, HPG, P])
        W = m.sb("W", [P, HPG, P])
        xdb = m.sb("xdb", [P, UN])
        yo = m.sb("yo", [P, H8, HD])
        xD = m.sb("xD", [P, UN])
        sq = m.sb("sq", [P, UN])
        par = m.sb("par", [P, G, XT, 4])
        dsk = m.sb("dsk", [P, HEADS])
        ng = m.sb("ng", [P, YT])
        ident, le, ge = (m.sb(n, [P, P]) for n in ("ident", "le", "ge"))
        gt = m.sb("gt", [P, P], F32R)
        lt = m.sb("lt", [P, P], F32R)
        ones = m.sb("ones", [P, P])
        pP = [m.ps(f"pP{i}") for i in range(2)]
        pA = [m.ps(f"pA{i}") for i in range(2)]
        pT, pS, pY, pO = (m.ps(n) for n in ("pT", "pS", "pY", "pO"))

        wld = m.sem("wld")
        yst = [m.sem(f"yst{b}") for b in range(NBL)]
        tld = [m.sem("tld0"), m.sem("tld1")]
        (small, con, whs, wls, pj, pev, t0s, cv, tnh, sil, tA, evA, xdA, stA, scA, auh, aul, arg, ex, mm_,
         wch, yoff, yoS, yd, xdF, xDs, stF, scF, ysum, fin1, sqs, ssm, vr, rs, dg, bcs, fin, vch, tri, wfw) = map(m.sem, (
             "small", "con", "whs", "wls", "pj", "pev", "t0s", "cv", "tnh", "sil", "tA", "evA", "xdA", "stA",
             "scA", "auh", "aul", "arg", "ex", "mm", "wch", "yoff", "yoS", "yd", "xdF", "xDs", "stF", "scF",
             "ysum", "fin1", "sqs", "ssm", "vr", "rs", "dg", "bcs", "fin", "vch", "tri", "wfw"))
        block = ctx.enter_context(nc.Block())

        def norm_bank(c):
            return pT if c < NCH - 1 else pA[0]

        def xt(g, c):
            return X[:, g % 2, 0:PAIRS, ucol(c * P):ucol(c * P) + P]

        def heads(ap):
            return ap.rearrange("p (t h) c -> p t h c", t=PAIRS)

        def xth(g, c):
            return xt(g, c).rearrange("p t (h c) -> p t h c", c=HD)

        def col(g, which, c, lo, n=HPG):
            return tab[:, g % 2, which, c, lo:lo + n].unsqueeze(2).to_broadcast([P, n, HD])

        @block.sync
        def _(sp):
            def load(w):
                if w:
                    sp.wait_ge(wls, w)
                sp.dma_start(wr[:, :, :], a["w_ssd"][w]).then_inc(wld, 16)

            load(0)
            for dst, src in ((par, "conv"), (ng, "norm_g"), (ident, "ident"), (le, "m_le"),
                             (ge, "m_ge")):
                sp.dma_start(dst[tuple(slice(None) for _ in dst.shape)], a[src]).then_inc(small, 16)

            sp.dma_start(dsk[:, :], a["dskip"].partition_broadcast(P)).then_inc(small, 16)

            def tables(g):
                sp.dma_start(tab[:, g % 2, :, :, :], tabs_dram[g]).then_inc(tld[g % 2], 16)

            def store(g):
                for b, (lo, hi) in enumerate(CHUNKS):
                    sp.wait_ge(fin, NCH * g + hi)
                    sp.dma_start(y_dram[:, PAIRS * g:PAIRS * (g + 1), lo * P:hi * P],
                                 Z[:, :, lo * P:hi * P]).then_inc(yst[b], 16)

            for w, (kind, g, i) in enumerate(tiles):
                if w:
                    load(w)
                if w == 1:
                    tables(0)
                    tables(1)
                if kind == "z" and i == PAIRS - 1 and g >= 1:
                    store(g - 1)
                    if g + 1 < G:
                        tables(g + 1)
            store(G - 1)
            for b in range(NBL):
                sp.wait_ge(yst[b], 16 * G)

        @block.tensor
        def _(pe):
            def unit(q):
                w, b = divmod(q, NBL)
                t0, n = BLOCKS[b]
                pe.wait_ge(wls, w + 1)
                if q >= 2:
                    pe.wait_ge(pev, q - 1)
                project(pe, pP[q % 2][:, 0:n], whi[:, w % 2], wlo[:, w % 2], h_hi, h_lo, t0, n).then_inc(pj, 1)

            def args(g, c):
                i = g * NCH + c
                pe.wait_ge(auh, i + 1)
                pe.wait_ge(aul, i + 1)
                if i >= 2:
                    pe.wait_ge(ex, i - 1)
                if g and c == 0:
                    pe.wait_ge(fin, g * NCH)
                for d, after in enumerate((gt, lt)):
                    for part, au in enumerate((aUh, aUl)):
                        x = pe.matmul(pA[i % 2][:, :], after[:, :], au[:, d * HPG:(d + 1) * HPG, :]
                                      .rearrange("p h l -> p (h l)"), start=(d == 0 and part == 0),
                                      stop=(d == 1 and part == 1))
                x.then_inc(arg, 1)

            def back(g, i):
                c = BACK[i]
                n = g * NCH + i
                u0 = ucol(c * P)
                if c in (CCH - 1, NCH - 1):
                    pe.wait_ge(sil, x_unit(g, 0 if c < CCH else NBL - 1) + 1)
                if i == 0:
                    if g:
                        pe.wait_ge(vr, g * NCH - 2)
                        pe.wait_ge(fin, g * NCH - 3)
                if n:
                    pe.wait_ge(evA, n)
                for t in range(XT - 1):
                    pe.transpose(pT[:, t * P:(t + 1) * P], X[:, g % 2, t, u0:u0 + P], ident[:, :])
                pe.matmul(pT[:, 3 * P:4 * P], X[:, g % 2, B_, u0:u0 + P], X[:, g % 2, C_, u0:u0 + P],
                          start=True, stop=True).then_inc(tA, 1)

            def back_state(g, i):
                n = g * (NCH - 1) + i
                u0 = ucol(BACK[i] * P)
                pe.wait_ge(xdA, n + 1)
                if n:
                    pe.wait_ge(scA, n)
                if g:
                    pe.wait_ge(scF, g * (NCH - 1))
                pe.matmul(pS[:, 0:UN], X[:, g % 2, B_, u0:u0 + P], xdb[:, :], start=True, stop=True).then_inc(stA, 1)

            def forth(g, c):
                n = g * NCH + c
                u0 = ucol(c * P)
                if c:
                    pe.wait_ge(scF, g * (NCH - 1) + c)
                else:
                    pe.wait_ge(scA, (g + 1) * (NCH - 1))
                if n:
                    pe.wait_ge(yoS, n)
                prev = hf[:, :] if c else hz
                back = hb[:, c, :]
                pe.matmul(pO[:, 0:UN], X[:, g % 2, C_, u0:u0 + P], prev, start=True, stop=True)
                pe.matmul(pO[:, UN:2 * UN], X[:, g % 2, C_, u0:u0 + P], back, start=True,
                          stop=True).then_inc(yoff, 1)
                if c + 1 < NCH:
                    args(g, c + 1)
                pe.wait_ge(mm_, n + 1)
                pe.wait_ge(evA, (g + 1) * NCH)
                if n:
                    pe.wait_ge(fin1, n)
                for k in range(HPG):
                    r = (k % 2) * HD
                    x = pe.matmul(pY[r:r + HD, (k // 2) * P:(k // 2 + 1) * P],
                                  X[:, g % 2, k // 2, u0 + r:u0 + r + HD], E[:, n % 2, k, :], start=(k < 2),
                                  stop=False, skip_group_check=True)
                x.then_inc(yd, 1)
                if c + 1 < NCH:
                    pe.wait_ge(xdF, g * (NCH - 1) + c + 1)
                    if c:
                        pe.wait_ge(scF, g * (NCH - 1) + c)
                    pe.matmul(pS[:, 0:UN], X[:, g % 2, B_, u0:u0 + P], xdb[:, :], start=True,
                              stop=True).then_inc(stF, 1)

            def off_sum(g, c):
                n = g * NCH + c
                pe.wait_ge(yoS, n + 1)
                for t in range(PAIRS):
                    x = pe.matmul(pY[:, t * P:(t + 1) * P], yo[:, 2 * t:2 * t + 2, :].rearrange("p h c -> p (h c)"),
                                  ident[:, :], start=False, stop=(t == PAIRS - 1), skip_group_check=True)
                x.then_inc(ysum, 1)

            def norms(g, c):
                bank = norm_bank(c)
                n = g * NCH + c
                if 0 <= c - 2 < NCH:
                    pe.wait_ge(dg, n - 1)
                    if n >= 3:
                        pe.wait_ge(fin, n - 2)
                    if c == NCH - 1:
                        pe.wait_ge(ex, n)
                    pe.matmul(bank[:, P:2 * P], ones[:, :], diag[:, :], start=True, stop=True).then_inc(bcs, 1)
                if 0 <= c - 1 < NCH:
                    pe.wait_ge(sqs, n)
                    if n >= 2:
                        pe.wait_ge(vr, n - 1)
                    for t in range(PAIRS):
                        x = pe.matmul(bank[:, 0:1], sq[:, t * P:(t + 1) * P], ones[:, 0:1], start=(t == 0),
                                      stop=(t == PAIRS - 1))
                    x.then_inc(ssm, 1)

            for q in range(PRO):
                unit(q)
            pe.wait_ge(small, 96)
            pe.wait_ge(con, 7)
            for g in range(G):
                for i in range(NCH):
                    back(g, i)
                    if i == NCH - 1:
                        args(g, 0)
                    if units[g][i] is not None:
                        unit(units[g][i])
                    if i < NCH - 1:
                        back_state(g, i)
                    if g and i < 2:
                        norms(g - 1, NCH + i)
                for c in range(NCH):
                    forth(g, c)
                    if units[g][NCH + c] is not None:
                        unit(units[g][NCH + c])
                    off_sum(g, c)
                    norms(g, c)
            norms(G - 1, NCH)
            norms(G - 1, NCH + 1)

        @block.scalar
        def _(act):
            def split(w):
                act.wait_ge(wld, 16 * (w + 1))
                if w >= 2:
                    act.wait_ge(pj, NBL * (w - 1))
                act.activation(whi[:, w % 2, :, :], wr[:, :, :], ACT.Copy).then_inc(whs, 1)

            def take(q):
                w, b = divmod(q, NBL)
                kind, g, i = tiles[w]
                t0, n = BLOCKS[b]
                act.wait_ge(pj, q + 1)
                if kind == "x":
                    if x_before[q]:
                        act.wait_ge(cv, 2 * x_before[q - 1])
                    act.activation(u[:, ucol(t0):ucol(t0) + n], pP[q % 2][:, 0:n], ACT.Copy).then_inc(pev, 1)
                else:
                    if i == 0 and g:
                        act.wait_ge(yst[b], 16 * g)
                    act.activation(Z[:, i, t0:t0 + n], pP[q % 2][:, 0:n], ACT.Copy, scale=0.5).then_inc(pev, 1)
                if b == 0 and w + 1 < len(tiles):
                    split(w + 1)
                if kind == "x":
                    lo, hi = SPAN[b]
                    act.wait_ge(pev, q + 1)
                    act.activation(X[:, g % 2, i, lo:hi], u[:, lo:hi], ACT.Identity,
                                   bias=par[:, g, i, 3:4], scale=par[:, g, i, 1:2]).then_inc(t0s, 1)

            def gate(q):
                w, b = divmod(q, NBL)
                kind, g, i = tiles[w]
                if q:
                    act.wait_ge(sil, q)
                if kind == "x":
                    lo, hi = SPAN[b]
                    act.wait_ge(cv, 2 * (x_before[q] + 1))
                    src = X[:, g % 2, i, lo:hi]
                else:
                    lo, hi = BLOCKS[b][0], BLOCKS[b][0] + BLOCKS[b][1]
                    act.wait_ge(pev, q + 1)
                    src = Z[:, i, lo:hi]
                act.activation(th[:, 0:hi - lo], src, ACT.Tanh).then_inc(tnh, 1)

            def at(step, lag):
                return line[step - lag] if step >= lag else None

            def steps_hi(g, c):
                n = g * NCH + c
                if c == 0:
                    act.wait_ge(tld[g % 2], 16 * (g // 2 + 1))
                if n:
                    act.wait_ge(arg, n)
                for k in range(H8):
                    x = act.activation(aUh[:, k, :], (le if k < HPG else ge)[:, :], ACT.Copy,
                                       scale=tab[:, g % 2, A_HI, c, k:k + 1])
                x.then_inc(auh, 1)

            def back(g, i):
                c = BACK[i]
                u0 = ucol(c * P)
                n = g * NCH + i
                act.wait_ge(tA, n + 1)
                act.activation(X[:, g % 2, 0:XT - 1, u0:u0 + P], pT[:, 0:3 * P].rearrange("p (t c) -> p t c", c=P),
                               ACT.Copy)
                if g and i == 0:
                    act.wait_ge(tri, 2 * g * NCH)
                    act.wait_ge(wfw, g * NCH)
                act.activation(cb[:, c, :], pT[:, 3 * P:4 * P], ACT.Copy).then_inc(evA, 1)

            def forward_part(g, c):
                n = g * NCH + c
                act.wait_ge(tri, 2 * n + 2)
                if n:
                    act.wait_ge(mm_, n)
                for k in range(HPG):
                    x = act.activation(W[:, k, :], cb[:, c, :], ACT.Copy, scale=tab[:, g % 2, DT, c, k:k + 1])
                x.then_inc(wfw, 1)

            def decays(g, c):
                n = g * NCH + c
                act.wait_ge(arg, n + 1)
                if n >= 2:
                    act.wait_ge(yd, n - 1)
                act.activation(E[:, n % 2, :, :], pA[n % 2][:, :].rearrange("p (h l) -> p h l", l=P),
                               ACT.Exp).then_inc(ex, 1)

            def square(g, c):
                n = g * NCH + c
                act.wait_ge(fin1, n + 1)
                if n:
                    act.wait_ge(ssm, n)
                act.activation(sq[:, :].rearrange("p (t l) -> p t l", l=P), Z[:, :, c * P:(c + 1) * P],
                               ACT.Square).then_inc(sqs, 1)

            split(0)
            act.wait_ge(small, 96)
            act.wait_ge(con, 7)
            for step in range(PRO):
                if at(step, 2) is not None:
                    gate(at(step, 2))
                take(step)
            for g in range(G):
                for s in range(SLOTS):
                    step = PRO + g * SLOTS + s
                    c = s - NCH
                    if c < 0:
                        back(g, s)
                    if -1 <= c < NCH - 1:
                        forward_part(g, c + 1)
                    if -2 <= c < NCH - 2:
                        steps_hi(g, c + 2)
                    if -1 <= c < NCH - 1:
                        decays(g, c + 1)
                    if at(step, 2) is not None:
                        gate(at(step, 2))
                    if c > 0:
                        square(g, c - 1)
                    if g and s == 0:
                        square(g - 1, NCH - 1)
                    if at(step, 0) is not None:
                        take(at(step, 0))
            square(G - 1, NCH - 1)

        @block.gpsimd
        def _(pool):
            pool.memset(ones[:, :], 1.0).then_inc(con, 1)
            pool.memset(mhalf[:, :], -0.5).then_inc(con, 2)


            def split_lo(w):
                pool.wait_ge(whs, w + 1)
                pool.tensor_tensor(wlo[:, w % 2, :, :], wr[:, :, :], whi[:, w % 2, :, :].bitcast(F32),
                                   ALU.subtract).then_inc(wls, 1)

            def steps_lo(g, c):
                n = g * NCH + c
                if c == 0:
                    pool.wait_ge(tld[g % 2], 16 * (g // 2 + 1))
                if n:
                    pool.wait_ge(arg, n)
                for d, upto in enumerate((le, ge)):
                    x = pool.tensor_tensor(aUl[:, d * HPG:(d + 1) * HPG, :],
                                           upto[:, :].unsqueeze(1).to_broadcast([P, HPG, P]),
                                           tab[:, g % 2, A_LO, c, d * HPG:(d + 1) * HPG].unsqueeze(2)
                                           .to_broadcast([P, HPG, P]), ALU.mult)
                x.then_inc(aul, 1)

            def factor(g, c):
                pool.wait_ge(vr, g * NCH + c + 1)
                if g or c:
                    pool.wait_ge(dg, g * NCH + c)
                pool.tensor_tensor(rstd[:, :], var[:, :], mhalf[:, :], ALU.pow).then_inc(rs, 1)

            split_lo(0)
            for q in range(PRO):
                if q % NBL == 0:
                    split_lo(q // NBL + 1)
            pool.wait_ge(con, 7)
            pool.wait_ge(small, 96)
            for g in range(G):
                for s in range(SLOTS):
                    c = s - NCH
                    if c >= 2:
                        factor(g, c - 2)
                    if g and s < 2:
                        factor(g - 1, NCH - 2 + s)
                    if c < 0 and s < NCH - 1:
                        n = g * (NCH - 1) + s
                        pool.wait_ge(evA, g * NCH + s + 1)
                        if s == 0:
                            pool.wait_ge(tld[g % 2], 16 * (g // 2 + 1))
                            if g:
                                pool.wait_ge(stF, g * (NCH - 1))
                        if n:
                            pool.wait_ge(stA, n)
                        cc = BACK[s]
                        pool.tensor_tensor(heads(xdb[:, :].rearrange("p (h c) -> p h c", c=HD)), xth(g, cc),
                                           heads(col(g, DTDEC, cc, HPG)), ALU.mult).then_inc(xdA, 1)
                    if c == 0:
                        pool.wait_ge(evA, (g + 1) * NCH)
                    if c >= 0:
                        if c + 1 < NCH:
                            n = g * (NCH - 1) + c
                            if c == 0:
                                pool.wait_ge(stA, (g + 1) * (NCH - 1))
                            if n:
                                pool.wait_ge(stF, n)
                            pool.tensor_tensor(heads(xdb[:, :].rearrange("p (h c) -> p h c", c=HD)), xth(g, c),
                                               heads(col(g, DTDEC, c, 0)), ALU.mult).then_inc(xdF, 1)
                        n = g * NCH + c
                        if n:
                            pool.wait_ge(yoS, n)
                        pool.tensor_tensor(heads(xD[:, :].rearrange("p (h c) -> p h c", c=HD)), xth(g, c),
                                           heads(dsk[:, g * HPG:(g + 1) * HPG].unsqueeze(2)
                                                 .to_broadcast([P, HPG, HD])), ALU.mult).then_inc(xDs, 1)
                    if -2 <= c < NCH - 2:
                        steps_lo(g, c + 2)
                    q = units[g][s]
                    if q is not None and q % NBL == 0 and q // NBL + 1 < len(tiles):
                        split_lo(q // NBL + 1)
            factor(G - 1, NCH - 2)
            factor(G - 1, NCH - 1)

        @block.vector
        def _(dve):
            n_ch = [0]

            def chain(x):
                x.then_inc(vch, 1)
                n_ch[0] += 1
                dve.wait_ge(vch, n_ch[0])

            for x in (dve.memset(u[:, :], 0.0), dve.memset(hz, 0.0)):
                x.then_inc(con, 1)
            dve.wait_ge(small, 96)
            chain(dve.tensor_scalar(par[:, :, :, :], par[:, :, :, :], 0.5, None, ALU.mult))
            dve.tensor_scalar(gt[:, :], le[:, :], -1.0, 1.0, ALU.mult, ALU.add).then_inc(con, 1)
            dve.tensor_scalar(lt[:, :], ge[:, :], -1.0, 1.0, ALU.mult, ALU.add).then_inc(con, 1)

            def conv(q):
                w, b = divmod(q, NBL)
                kind, g, i = tiles[w]
                if kind != "x":
                    return
                n = x_before[q]
                lo, hi = SPAN[b]
                dve.wait_ge(t0s, n + 1)
                o = X[:, g % 2, i, lo:hi]
                dve.scalar_tensor_tensor(o, u[:, lo - 1:hi - 1], par[:, g, i, 0:1], o, ALU.mult, ALU.add
                                         ).then_inc(cv, 1)
                dve.wait_ge(cv, 2 * n + 1)
                dve.scalar_tensor_tensor(o, u[:, lo + 1:hi + 1], par[:, g, i, 2:3], o, ALU.mult, ALU.add
                                         ).then_inc(cv, 1)

            def silu(q):
                w, b = divmod(q, NBL)
                kind, g, i = tiles[w]
                dve.wait_ge(tnh, q + 1)
                if kind == "x":
                    lo, hi = SPAN[b]
                    o = X[:, g % 2, i, lo:hi]
                else:
                    lo, hi = BLOCKS[b][0], BLOCKS[b][0] + BLOCKS[b][1]
                    o = Z[:, i, lo:hi]
                dve.scalar_tensor_tensor(o, th[:, 0:hi - lo], 1.0, o, ALU.add, ALU.mult).then_inc(sil, 1)

            def at(step, lag):
                return line[step - lag] if step >= lag else None

            def h3(ap):
                return ap.rearrange("p (h c) -> p h c", c=HD)

            def back(g, i):
                if i == NCH - 1:
                    return
                n = g * (NCH - 1) + i
                c, nxt = BACK[i], BACK[i + 1]
                if i == 0 and g:
                    dve.wait_ge(yoff, g * NCH)
                if i == 0:
                    dve.wait_ge(tld[g % 2], 16 * (g // 2 + 1))
                if n:
                    dve.wait_ge(scA, n)
                chain(dve.tensor_tensor(h3(hb[:, nxt, :]), h3(hb[:, c, :] if i else hz),
                                        col(g, ETOT, c, HPG), ALU.mult))
                dve.wait_ge(stA, n + 1)
                dve.tensor_tensor(hb[:, nxt, :], hb[:, nxt, :], pS[:, 0:UN], ALU.add).then_inc(scA, 1)

            def triangles(g, c):
                n = g * NCH + c
                dve.wait_ge(evA, g * NCH + CCH if c < CCH else (g + 1) * NCH)
                if n:
                    dve.wait_ge(wch, n)
                dve.tensor_tensor(cbm[:, :], cb[:, c, :], ge[:, :], ALU.mult).then_inc(tri, 1)
                dve.wait_ge(tri, 2 * n + 1)
                dve.tensor_tensor(cb[:, c, :], cb[:, c, :], le[:, :], ALU.mult).then_inc(tri, 1)

            def masked(g, c):
                n = g * NCH + c
                dve.wait_ge(wfw, n + 1)
                dve.wait_ge(tri, 2 * n + 2)
                for k in range(HPG):
                    x = dve.scalar_tensor_tensor(W[:, k, :], cbm[:, :], tab[:, g % 2, DT, c, HPG + k:HPG + k + 1],
                                                 W[:, k, :], ALU.mult, ALU.add)
                x.then_inc(wch, 1)

            def times_decay(g, c):
                n = g * NCH + c
                dve.wait_ge(ex, n + 1)
                dve.wait_ge(wch, n + 1)
                dve.tensor_tensor(E[:, n % 2, :, :], E[:, n % 2, :, :], W[:, :, :], ALU.mult).then_inc(mm_, 1)

            def offs(g, c):
                n = g * NCH + c
                dve.wait_ge(yoff, n + 1)
                if n:
                    dve.wait_ge(ysum, n)
                chain(dve.tensor_tensor(yo[:, :, :], pO[:, :].rearrange("p (h c) -> p h c", c=HD),
                                        col(g, ECUM, c, 0, H8), ALU.mult))
                chain(dve.tensor_tensor(yo[:, 0:HPG, :], yo[:, 0:HPG, :], yo[:, HPG:H8, :], ALU.add))
                dve.wait_ge(xDs, n + 1)
                dve.tensor_tensor(yo[:, 0:HPG, :], yo[:, 0:HPG, :], h3(xD[:, :]), ALU.add).then_inc(yoS, 1)

            def scan(g, c):
                if c == NCH - 1:
                    return
                n = g * (NCH - 1) + c
                prev = hf[:, :] if c else hz
                nxt = hf[:, :]
                if n:
                    dve.wait_ge(scF, n)
                chain(dve.tensor_tensor(h3(nxt), h3(prev), col(g, ETOT, c, 0), ALU.mult))
                dve.wait_ge(stF, n + 1)
                dve.tensor_tensor(nxt, nxt, pS[:, 0:UN], ALU.add).then_inc(scF, 1)

            def gated(g, c):
                n = g * NCH + c
                dve.wait_ge(ysum, n + 1)
                dve.wait_ge(sil, z_unit(g, block_of[c]) + 1)
                zc = Z[:, :, c * P:(c + 1) * P]
                dve.tensor_tensor(zc, pY[:, 0:UN].rearrange("p (t l) -> p t l", l=P), zc, ALU.mult).then_inc(fin1, 1)

            def norm_early(g, c):
                n = g * NCH + c
                if 0 <= c - 2 < NCH:
                    dve.wait_ge(ssm, n - 1)
                    if n >= 3:
                        dve.wait_ge(rs, n - 2)
                    dve.tensor_scalar(var[:, :], norm_bank(c - 1)[:, 0:1], 1.0 / UN, EPS, ALU.mult,
                                      ALU.add).then_inc(vr, 1)
                if 0 <= c - 3 < NCH:
                    dve.wait_ge(bcs, n - 2)
                    for t in range(PAIRS):
                        zt = Z[:, t, (c - 3) * P:(c - 2) * P]
                        x = dve.scalar_tensor_tensor(zt, zt, ng[:, g * PAIRS + t:g * PAIRS + t + 1],
                                                     norm_bank(c - 1)[:, P:2 * P], ALU.mult, ALU.mult)
                    x.then_inc(fin, 1)

            def norm_late(g, c):
                n = g * NCH + c
                if 0 <= c - 2 < NCH:
                    dve.wait_ge(rs, n - 1)
                    if n >= 3:
                        dve.wait_ge(bcs, n - 2)
                    dve.tensor_scalar(diag[:, :], ident[:, :], rstd[:, 0:1], None, ALU.mult).then_inc(dg, 1)

            for step in range(PRO):
                if at(step, 1) is not None:
                    conv(at(step, 1))
                if at(step, 2) is not None:
                    silu(at(step, 2))
            for g in range(G):
                for s in range(SLOTS):
                    step = PRO + g * SLOTS + s
                    c = s - NCH
                    if g and s < 3:
                        norm_early(g - 1, NCH + s)
                    if c >= 0:
                        norm_early(g, c)
                    if c < 0:
                        back(g, s)
                    else:
                        offs(g, c)
                        scan(g, c)
                    if g and s < 2:
                        norm_late(g - 1, NCH + s)
                    if c >= 0:
                        norm_late(g, c)
                    if -1 <= c < NCH - 1:
                        masked(g, c + 1)
                        times_decay(g, c + 1)
                    if -2 <= c < NCH - 2:
                        triangles(g, c + 2)
                    if at(step, 1) is not None:
                        conv(at(step, 1))
                    if c >= 0:
                        gated(g, c)
                    if at(step, 2) is not None:
                        silu(at(step, 2))
            for c in range(NCH, NCH + 3):
                norm_early(G - 1, c)
                norm_late(G - 1, c)


def out_project(nc, a, layer, y_dram, kt, w_dram, tiles, mod_rows, st_o):
    NH = D // 2
    with ExitStack() as ctx:
        m = Mem(nc, ctx, f"op{layer}")
        whi = m.sb("whi", [P, kt, D], F32R)
        wlo = m.sb("wlo", [P, kt, D], F32R)
        RW = 4
        wr = m.sb("wr", [P, RW, D])
        x = wr[:, 2:4, :]
        yr = m.sb("yr", [P, 2, kt, P])
        yhi = m.sb("yhi", [P, 2, kt, P], F32R)
        ylo = m.sb("ylo", [P, 2, kt, P], F32R)
        o = m.sb("o", [P, D])
        G = m.sb("G", [P, 2, D])
        st = m.sb("st", [P, 2])
        var = m.sb("var", [P, 1])
        rstd = m.sb("rstd", [P, 1])
        mhalf = m.sb("mhalf", [P, 1])
        pa = [[m.ps(f"pa{i}{h}") for h in range(2)] for i in range(2)]
        wl = [m.sem(f"wl{i}") for i in range(RW)]
        yl = [m.sem("yl0"), m.sem("yl1")]
        xl = [m.sem("xl0"), m.sem("xl1")]
        gl, gg, whs, wls, yhs, yls, mm_, sqs, vr, rs, sc, ad, con = map(m.sem, (
            "gl", "gg", "whs", "wls", "yhs", "yls", "mm", "sqs", "vr", "rs", "sc", "ad", "con"))
        block = ctx.enter_context(nc.Block())
        N = len(tiles)

        @block.sync
        def _(sp):
            def load_y(t):
                if t >= 2:
                    sp.wait_ge(yls, t - 1)
                c0 = tiles[t][0]
                sp.dma_start(yr[:, t % 2, :, :], y_dram[:, :, c0:c0 + P]).then_inc(yl[t % 2], 16)

            for k in range(kt):
                if k >= RW:
                    sp.wait_ge(wls, k - RW + 1)
                sp.dma_start(wr[:, k % RW, :], w_dram[k * P:(k + 1) * P, :]).then_inc(wl[k % RW], 16)
                if k < 2:
                    load_y(k)
            sp.dma_start(o[:, :], a["post_g"][layer].partition_broadcast(P)).then_inc(gl, 16)
            for v in range(2):
                sp.dma_start(G[:, v, :], mod_rows[v, layer, 2 * D:3 * D].partition_broadcast(P)).then_inc(gl, 16)
            sp.wait_ge(wls, kt)
            for t in range(N):
                if t >= 2:
                    sp.wait_ge(ad, t - 1)
                (dst, src) = tiles[t][2](x[:, t % 2, :])
                sp.dma_start(dst, src).then_inc(xl[t % 2], 16)
                if t >= 1:
                    if t + 1 < N:
                        load_y(t + 1)
                    sp.wait_ge(ad, t)
                    (dst, src) = tiles[t - 1][3](o[:, :])
                    sp.dma_start(dst, src).then_inc(st_o, 16)
            sp.wait_ge(ad, N)
            (dst, src) = tiles[N - 1][3](o[:, :])
            sp.dma_start(dst, src).then_inc(st_o, 16)
            sp.wait_ge(st_o, 16 * N)

        @block.tensor
        def _(pe):
            def products(t, k):
                for y, ws in ((yhi, (whi, wlo)), (ylo, (whi,))):
                    for w in ws:
                        for h in range(2):
                            z = pe.matmul(pa[t % 2][h][:, :], y[:, t % 2, k, :], w[:, k, h * NH:(h + 1) * NH],
                                          start=(k == 0 and y is yhi and w is whi),
                                          stop=(k == kt - 1 and y is ylo))
                if k == kt - 1:
                    z.then_inc(mm_, 1)

            for k in range(kt):
                pe.wait_ge(wls, k + 1)
                for t in range(2):
                    if k == 0:
                        pe.wait_ge(yls, t + 1)
                    products(t, k)
            for t in range(2, N):
                pe.wait_ge(yls, t + 1)
                pe.wait_ge(sc, 2 * (t - 1))
                for k in range(kt):
                    products(t, k)

        @block.scalar
        def _(act):
            def y_hi(t):
                act.wait_ge(yl[t % 2], 16 * (t // 2 + 1))
                if t >= 2:
                    act.wait_ge(mm_, t - 1)
                act.activation(yhi[:, t % 2, :, :], yr[:, t % 2, :, :], ACT.Copy).then_inc(yhs, 1)

            for k in range(kt):
                act.wait_ge(wl[k % RW], 16 * (k // RW + 1))
                act.activation(whi[:, k, :], wr[:, k % RW, :], ACT.Copy).then_inc(whs, 1)
                if k < 2:
                    y_hi(k)
            for t in range(N):
                act.wait_ge(mm_, t + 1)
                if t:
                    act.wait_ge(st_o, 16 * t)
                else:
                    act.wait_ge(gg, 1)
                for h in range(2):
                    z = act.activation(o[:, h * NH:(h + 1) * NH], pa[t % 2][h][:, :], ACT.Square,
                                       accum_out=st[:, h:h + 1])
                z.then_inc(sqs, 1)
                if t + 2 < N:
                    y_hi(t + 2)

        @block.gpsimd
        def _(pool):
            pool.memset(mhalf[:, :], -0.5).then_inc(con, 1)
            pool.wait_ge(con, 1)
            for t in range(N):
                pool.wait_ge(vr, 2 * t + 2)
                pool.tensor_tensor(rstd[:, :], var[:, :], mhalf[:, :], ALU.pow).then_inc(rs, 1)

        @block.vector
        def _(dve):
            def y_lo(t):
                dve.wait_ge(yhs, t + 1)
                dve.tensor_tensor(ylo[:, t % 2, :, :], yr[:, t % 2, :, :], yhi[:, t % 2, :, :].bitcast(F32),
                                  ALU.subtract).then_inc(yls, 1)

            for k in range(kt):
                dve.wait_ge(whs, k + 1)
                dve.tensor_tensor(wlo[:, k, :], wr[:, k % RW, :], whi[:, k, :].bitcast(F32),
                                  ALU.subtract).then_inc(wls, 1)
                if k < 2:
                    y_lo(k)
            dve.wait_ge(gl, 48)
            dve.tensor_tensor(G[:, :, :], G[:, :, :], o[:, :].unsqueeze(1).to_broadcast([P, 2, D]),
                              ALU.mult).then_inc(gg, 1)
            for t in range(N):
                v = 1 if tiles[t][1] else 0
                dve.wait_ge(sqs, t + 1)
                dve.tensor_tensor(var[:, :], st[:, 0:1], st[:, 1:2], ALU.add).then_inc(vr, 1)
                dve.wait_ge(vr, 2 * t + 1)
                dve.tensor_scalar(var[:, :], var[:, :], 1.0 / D, EPS, ALU.mult, ALU.add).then_inc(vr, 1)
                dve.wait_ge(rs, t + 1)
                if t == 0:
                    dve.wait_ge(gg, 1)
                for h in range(2):
                    dve.scalar_tensor_tensor(o[:, h * NH:(h + 1) * NH], pa[t % 2][h][:, :], rstd[:, 0:1],
                                             G[:, v, h * NH:(h + 1) * NH], ALU.mult, ALU.mult).then_inc(sc, 1)
                dve.wait_ge(sc, 2 * (t + 1))
                dve.wait_ge(xl[t % 2], 16 * (t // 2 + 1))
                dve.tensor_tensor(o[:, :], o[:, :], x[:, t % 2, :], ALU.add).then_inc(ad, 1)
                if t + 2 < N:
                    y_lo(t + 2)


GW, WR, WC = 64, 8, 16
GR = SEQ // GW
NAH, NAD = 16, 64
QR, QC = 8, 16
RB, CB = GR // QR, GW // QC
KR, KC = 12, 32
DR, DC = 2 * WR - 1, 2 * WC - 1
K0C = [min(max(QC * c - WC // 2, 0), GW - KC) for c in range(CB)]
NEG = -1e30
PADW = 64


def key_row0(rb):
    return (WR // 2) * rb


def row_start(r):
    return min(max(r - WR // 2, 0), GR - WR)


def attention(nc, a, h_hi, h_lo, bt_dram, y_dram):
    PR = NAH // 2
    QT = RB * CB
    UP = 2 * QT
    NU = PR * UP
    NW, NC_ = KR * KC, CTX
    NK = NW + NC_
    JW, JC = NW // P, NC_ // P
    WIN = CB * (GR // 4)
    KINDS = "vkqg"
    ublocks = {"v": (0, 1, 2), "k": (0, 1, 2), "q": (1, 2), "g": (1, 2)}
    units = [(p, i, kd, b) for p in range(PR) for i, kd in enumerate(KINDS) for b in ublocks[kd]]
    UPP = len(units) // PR
    ksteps = [(i, k, BLOCKS[units[i][3]][1]) for i in range(UPP) for k in range(KT)]
    total = sum(n for _, _, n in ksteps)
    before = [sum(n for _, _, n in ksteps[:j]) for j in range(len(ksteps))]
    place = [[(i, k) for (i, k, _), b in zip(ksteps, before) if b * UP // total == r] for r in range(UP)]
    ends = [[i for i, k in slot if k == KT - 1] for slot in place]
    done = {}
    for q, (p, i, kd, b) in enumerate(units):
        done[p, kd] = q + 1
    VG = -(-(WIN + JC) // 4)
    VS = UP - VG

    with ExitStack() as ctx:
        m = Mem(nc, ctx, "at")
        wr = m.sb("wr", [P, 2, KT, P])
        whi = m.sb("whi", [P, 2, KT, P], F32R)
        wlo = m.sb("wlo", [P, 2, KT, P], F32R)
        q2 = m.sb("q2", [P, 2, 2, SEQ])
        kk = m.sb("kk", [P, 2, TOK])
        vv = m.sb("vv", [P, WIN + JC, P])
        vt = m.sb("vt", [P, 2, WIN + JC, P])
        gg = m.sb("gg", [P, 2, SEQ])
        th = m.sb("th", [P, SEQ])
        bias = m.sb("bias", [P, RB, 2, CB, KR, KC])
        s = m.sb("s", [P, 2, NW])
        pm = m.sb("pm", [P, 2, NK])
        ptr = m.sb("ptr", [P, 2, JW + JC, P])
        ident = m.sb("ident", [P, P])
        mx = m.sb("mx", [P, 2, 2])
        nm = m.sb("nm", [P, 2])
        lsum = m.sb("lsum", [P, 2, 2])
        li = m.sb("li", [P, 2])
        pP = [m.ps(f"pP{i}") for i in range(2)]
        pA, pB, pT0, pT1, pO = (m.ps(n) for n in ("pA", "pB", "pT0", "pT1", "pO"))
        wld = [m.sem("wld0"), m.sem("wld1")]
        bl = [m.sem("bl0"), m.sem("bl1")]
        (small, con, whs, wls, pj, pev, tnh, gs, sc, mxs, nms, exs, ls, pn, tr, pt0, pt1, pv, ga, vtr, vte,
         yst) = map(m.sem, (
             "small", "con", "whs", "wls", "pj", "pev", "tnh", "gs", "sc", "mxs", "nms", "exs", "ls", "pn", "tr",
             "pt0", "pt1", "pv", "ga", "vtr", "vte", "yst"))
        block = ctx.enter_context(nc.Block())
        bview = bt_dram.rearrange("(c q) (h r) k -> q h c (r k)", c=CB, r=DR)

        def grid(ap):
            return ap[:, CTX:TOK].rearrange("p (r c) -> p r c", c=GW)

        def rest(n):
            p, r = divmod(n, UP)
            qt, e = divmod(r, 2)
            return p, qt, e, qt // CB, qt % CB

        def win_index(rb, cb, j):
            return cb * (GR // 4) + rb + j if j < JW else WIN + j - JW

        @block.sync
        def _(sp):
            def load_bias(p, rb):
                if p == 0:
                    sp.wait_ge(con, 1)
                if p:
                    sp.wait_ge(mxs, p * UP - UP + (rb + 1) * UP // RB)
                for e in range(2):
                    for qr in range(QR):
                        r = rb * QR + qr
                        k0 = row_start(r) - key_row0(rb)
                        d0 = row_start(r) - r + WR - 1
                        sp.dma_start(bias[qr * QC:(qr + 1) * QC, rb, e, :, k0:k0 + WR, :]
                                     .rearrange("q c r k -> q c (r k)"),
                                     bview[:, 2 * p + e, :, d0 * KC:(d0 + WR) * KC]).then_inc(bl[rb], 16)

            w = 0
            for p in range(PR + 1):
                for i in range(len(KINDS)):
                    if p < PR:
                        if w >= 2:
                            sp.wait_ge(wls, w - 1)
                        sp.dma_start(wr[:, w % 2, :, :], a["w_na"][w]).then_inc(wld[w % 2], 16)
                        w += 1
                    if p == 0 and i == 1:
                        sp.dma_start(ident[:, :], a["ident"]).then_inc(small, 16)
                    if p == 0 and i in (1, 2):
                        load_bias(0, i - 1)
                    if i == 1 and p >= 2:
                        sp.wait_ge(ga, QT * (p - 1))
                        sp.dma_start(y_dram[:, p - 2, :], gg[:, p % 2, :]).then_inc(yst, 16)
                        load_bias(p - 1, 1)
                    if i == 3 and 1 <= p < PR:
                        load_bias(p, 0)
            sp.wait_ge(ga, QT * PR)
            sp.dma_start(y_dram[:, PR - 1, :], gg[:, (PR - 1) % 2, :]).then_inc(yst, 16)
            sp.wait_ge(yst, 16 * PR)

        @block.tensor
        def _(pe):
            def unit(q, ks=range(KT)):
                p, i, kd, b = units[q]
                w = p * len(KINDS) + i
                t0, n = BLOCKS[b]
                if ks[0] == 0:
                    pe.wait_ge(wls, w + 1)
                    if q >= 2:
                        pe.wait_ge(pev, q - 1)
                x = project(pe, pP[q % 2][:, 0:n], whi[:, w % 2], wlo[:, w % 2], h_hi, h_lo, t0, n, ks)
                if ks[-1] == KT - 1:
                    x.then_inc(pj, 1)

            def scores(n):
                p, qt, e, rb, cb = rest(n)
                if n % UP == 0:
                    pe.wait_ge(pev, done[p, "q"])
                if n:
                    pe.wait_ge(exs, n)
                lhs = q2[:, p % 2, e, qt * P:(qt + 1) * P]
                r0 = key_row0(rb)
                pe.matmul(pA[:, 0:NW].rearrange("p (r c) -> p r c", c=KC), lhs,
                          grid(kk[:, p % 2, :])[:, r0:r0 + KR, K0C[cb]:K0C[cb] + KC], start=True, stop=True)
                pe.matmul(pB[:, 0:NC_], lhs, kk[:, p % 2, 0:CTX], start=True, stop=True).then_inc(sc, 1)

            def turn(n, vgroups):
                pe.wait_ge(pn, n + 1)
                if n:
                    pe.wait_ge(pt0, n)
                    pe.wait_ge(pt1, n)
                pe.wait_ge(vte, vgroups)
                for j in range(JW + JC):
                    bank, c = (pT0, j) if j < 4 else (pT1, j - 4)
                    x = pe.transpose(bank[:, c * P:(c + 1) * P], pm[:, n % 2, j * P:(j + 1) * P], ident[:, :])
                x.then_inc(tr, 1)

            def values(n):
                p, qt, e, rb, cb = rest(n)
                pe.wait_ge(pt0, n + 1)
                pe.wait_ge(pt1, n + 1)
                if n >= 2:
                    pe.wait_ge(ga, n // 2)
                for j in range(JW + JC):
                    x = pe.matmul(pO[e * NAD:(e + 1) * NAD, 0:P],
                                  vt[:, p % 2, win_index(rb, cb, j), e * NAD:(e + 1) * NAD],
                                  ptr[:, n % 2, j, :], start=(j == 0), stop=(j == JW + JC - 1))
                x.then_inc(pv, 1)

            def turn_values(p, gidx, turns):
                if gidx == 0:
                    pe.wait_ge(pev, done[p, "v"])
                if turns:
                    pe.wait_ge(pt0, turns)
                v = p * VG + gidx
                if v:
                    pe.wait_ge(vte, v)
                for c, j in enumerate(range(4 * gidx, min(4 * gidx + 4, WIN + JC))):
                    x = pe.transpose(pT0[:, c * P:(c + 1) * P], vv[:, j, :], ident[:, :])
                x.then_inc(vtr, 1)

            for q in range(UPP):
                unit(q)
            pe.wait_ge(small, 16)
            for gidx in range(VG):
                turn_values(0, gidx, 0)
            groups = VG
            for n in range(NU):
                p, r = divmod(n, UP)
                scores(n)
                if p + 1 < PR:
                    for i in sorted({i for i, k in place[r]}):
                        unit((p + 1) * UPP + i, [k for j, k in place[r] if j == i])
                if n:
                    turn(n - 1, groups)
                if n >= 2:
                    values(n - 2)
                if r >= VS and p + 1 < PR:
                    turn_values(p + 1, r - VS, n)
                    groups += 1
            turn(NU - 1, groups)
            values(NU - 2)
            values(NU - 1)

        @block.scalar
        def _(act):
            def split(w):
                act.wait_ge(wld[w % 2], 16 * (w // 2 + 1))
                if w >= 2:
                    p, i = divmod(w - 2, len(KINDS))
                    act.wait_ge(pj, done[p, KINDS[i]])
                act.activation(whi[:, w % 2, :, :], wr[:, w % 2, :, :], ACT.Copy).then_inc(whs, 1)

            def take(q):
                p, i, kd, b = units[q]
                w = p * len(KINDS) + i
                t0, n = BLOCKS[b]
                act.wait_ge(pj, q + 1)
                src = pP[q % 2]
                if kd == "k":
                    x = act.activation(kk[:, p % 2, t0:t0 + n], src[:, 0:n], ACT.Copy)
                elif kd == "v":
                    if b == 0 and p:
                        act.wait_ge(vtr, p * VG)
                    if b == 0:
                        x = act.activation(vv[:, WIN:WIN + JC, :], src[:, 0:n].rearrange("p (j c) -> p j c", c=P),
                                           ACT.Copy)
                    else:
                        rows = src[:, 0:n].rearrange("p (r c) -> p r c", c=GW)
                        for cw in range(CB):
                            j = cw * (GR // 4) + (b - 1) * (QR // 4)
                            x = act.activation(vv[:, j:j + QR // 4, :].rearrange("p j (r c) -> p (j r) c", c=KC),
                                               rows[:, :, K0C[cw]:K0C[cw] + KC], ACT.Copy)
                else:
                    rb = b - 1
                    view = src[:, 0:n].rearrange("p (r c q) -> p r c q", c=CB, q=QC)

                    def tiles(ap):
                        return ap[:, rb * CB * P:(rb + 1) * CB * P].rearrange("p (c r q) -> p r c q", c=CB, q=QC)
                    if kd == "q":
                        if q < UPP:
                            act.wait_ge(con, 2)
                        for e in range(2):
                            lo = e * NAD
                            x = act.activation(tiles(q2[lo:lo + NAD, p % 2, e, :]), view[lo:lo + NAD], ACT.Copy,
                                               scale=NAD ** -0.5)
                    else:
                        if b == 1 and p >= 2:
                            act.wait_ge(yst, 16 * (p - 1))
                        x = act.activation(tiles(gg[:, p % 2, :]), view, ACT.Copy, scale=0.5)
                x.then_inc(pev, 1)
                if b == ublocks[kd][0] and w + 1 < PR * len(KINDS):
                    split(w + 1)
                if kd == "g" and b == 2:
                    act.wait_ge(pev, q + 1)
                    if p:
                        act.wait_ge(gs, p)
                    act.activation(th[:, :], gg[:, p % 2, :], ACT.Tanh).then_inc(tnh, 1)

            def exps(n):
                act.wait_ge(nms, n + 1)
                if n >= 2:
                    act.wait_ge(tr, n - 1)
                act.activation(pm[:, n % 2, 0:NW], s[:, n % 2, :], ACT.Exp, bias=nm[:, n % 2:n % 2 + 1],
                               accum_out=lsum[:, n % 2, 0:1])
                act.activation(pm[:, n % 2, NW:NK], pB[:, 0:NC_], ACT.Exp, bias=nm[:, n % 2:n % 2 + 1],
                               accum_out=lsum[:, n % 2, 1:2]).then_inc(exs, 1)

            def keep_turned(n):
                act.wait_ge(tr, n + 1)
                if n >= 2:
                    act.wait_ge(pv, n - 1)
                act.activation(ptr[:, n % 2, 0:4, :], pT0[:, :].rearrange("p (j c) -> p j c", c=P),
                               ACT.Copy).then_inc(pt0, 1)

            def keep_values(p, gidx):
                act.wait_ge(vtr, p * VG + gidx + 1)
                j = 4 * gidx
                n = min(4, WIN + JC - j)
                act.activation(vt[:, p % 2, j:j + n, :], pT0[:, 0:n * P].rearrange("p (j c) -> p j c", c=P),
                               ACT.Copy).then_inc(vte, 1)

            split(0)
            for q in range(UPP):
                take(q)
            for gidx in range(VG):
                keep_values(0, gidx)
            for n in range(NU):
                p, r = divmod(n, UP)
                exps(n)
                if p + 1 < PR:
                    for i in ends[r]:
                        take((p + 1) * UPP + i)
                if n:
                    keep_turned(n - 1)
                if r >= VS and p + 1 < PR:
                    keep_values(p + 1, r - VS)
            keep_turned(NU - 1)

        @block.gpsimd
        def _(pool):
            for w in range(PR * len(KINDS)):
                pool.wait_ge(whs, w + 1)
                pool.tensor_tensor(wlo[:, w % 2, :, :], wr[:, w % 2, :, :], whi[:, w % 2, :, :].bitcast(F32),
                                   ALU.subtract).then_inc(wls, 1)

        @block.vector
        def _(dve):
            def gate_silu(p):
                dve.wait_ge(tnh, p + 1)
                dve.scalar_tensor_tensor(gg[:, p % 2, :], th[:, :], 1.0, gg[:, p % 2, :], ALU.add,
                                         ALU.mult).then_inc(gs, 1)

            def maxima(n):
                p, qt, e, rb, cb = rest(n)
                dve.wait_ge(sc, n + 1)
                if n % UP == rb * UP // RB:
                    dve.wait_ge(bl[rb], 16 * 2 * QR * (p + 1))
                if n >= 2:
                    dve.wait_ge(exs, n - 1)
                dve.tensor_tensor_reduce(s[:, n % 2, :], pA[:, 0:NW], bias[:, rb, e, cb, :, :]
                                         .rearrange("p r k -> p (r k)"), 1.0, -3e38, ALU.add, ALU.max,
                                         mx[:, n % 2, 0:1]).then_inc(mxs, 1)
                dve.tensor_reduce(mx[:, n % 2, 1:2], pB[:, 0:NC_], AX_X, ALU.max).then_inc(ls, 1)
                dve.wait_ge(mxs, n + 1)
                dve.wait_ge(ls, 3 * n + 1)
                dve.tensor_scalar(nm[:, n % 2:n % 2 + 1], mx[:, n % 2, 0:1], mx[:, n % 2, 1:2], -1.0, ALU.max,
                                  ALU.mult).then_inc(nms, 1)

            def normed(n):
                dve.wait_ge(exs, n + 1)
                dve.tensor_tensor(li[:, n % 2:n % 2 + 1], lsum[:, n % 2, 0:1], lsum[:, n % 2, 1:2],
                                  ALU.add).then_inc(ls, 1)
                dve.wait_ge(ls, 3 * n + 2)
                dve.reciprocal(li[:, n % 2:n % 2 + 1], li[:, n % 2:n % 2 + 1]).then_inc(ls, 1)
                dve.wait_ge(ls, 3 * n + 3)
                dve.tensor_scalar(pm[:, n % 2, :], pm[:, n % 2, :], li[:, n % 2:n % 2 + 1], None,
                                  ALU.mult).then_inc(pn, 1)

            def keep_turned(n):
                dve.wait_ge(tr, n + 1)
                if n >= 2:
                    dve.wait_ge(pv, n - 1)
                dve.tensor_copy(ptr[:, n % 2, 4, :], pT1[:, 0:P]).then_inc(pt1, 1)

            def gated(n):
                p, qt, e, rb, cb = rest(n)
                if e == 0:
                    return
                dve.wait_ge(pv, n + 1)
                if qt == 0:
                    dve.wait_ge(gs, p + 1)
                o = gg[:, p % 2, qt * P:(qt + 1) * P]
                dve.tensor_tensor(o, pO[:, 0:P], o, ALU.mult).then_inc(ga, 1)

            dve.memset(bias[:, :, :, :, :, :], NEG).then_inc(con, 1)
            dve.memset(q2[:, :, :, :], 0.0).then_inc(con, 1)
            gate_silu(0)
            for n in range(NU):
                p, r = divmod(n, UP)
                maxima(n)
                normed(n)
                if n:
                    keep_turned(n - 1)
                if n >= 2:
                    gated(n - 2)
                if r == UP - 1 and p + 1 < PR:
                    gate_silu(p + 1)
            keep_turned(NU - 1)
            gated(NU - 2)
            gated(NU - 1)


def program(nc, a, out, upto=None):
    stored = [nc.alloc_semaphore(f"stored{i}") for i in range(DEPTH)]
    mod_rows = nc.dram_tensor("mod_rows", [2, DEPTH, 3 * D], F32).ap()
    mod_cols = nc.dram_tensor("mod_cols", [P, DEPTH, 2 * KT, 2], F32).ap()
    tabs = nc.dram_tensor("tabs", [GROUPS, P, TABS, NCH, 2 * HPG], F32).ap()
    x1 = nc.dram_tensor("x1", [TOK, D], F32).ap()
    y1 = nc.dram_tensor("y1", [P, D // P, SEQ], F32).ap()
    pad = nc.dram_tensor("pad", [NAH * DR, PADW], F32).ap()
    run = nc.dram_tensor("run", [CB * QC, NAH * DR, KC], F32).ap()
    bt = nc.dram_tensor("bt", [CB * QC, NAH * DR, KC], F32).ap()
    y0 = nc.dram_tensor("y0", [P, YT, TOK], F32).ap()

    def x0(t):
        return a["ctx"][t * P:(t + 1) * P, :] if t < CCH else a["x"][(t - CCH) * P:(t - CCH + 1) * P, :]

    with ExitStack() as ctx:
        m = Mem(nc, ctx, "h0")
        csil = m.sb("csil", [P, KT, 2])
        first_modulation(nc, a, csil, [(0, c) for c in range(4)], mod_rows, mod_cols, pad, run)
        h_hi = m.sb("h_hi", [P, KT, TOK], F32R)
        h_lo = m.sb("h_lo", [P, KT, TOK], F32R)
        norm_transpose(nc, a, 0, x0, mod_cols, mod_rows, h_hi, h_lo, csil, [(0, 4), (0, 5), (1, 0), (1, 1)],
                       pad, run)
        time_steps(nc, a, h_hi, h_lo, tabs, csil, [(1, c) for c in range(2, 6)], mod_rows, mod_cols,
                   pad, run, bt)
        ssd_groups(nc, a, h_hi, h_lo, tabs, y0)

    def rows(ap, t):
        return ap[t * P:(t + 1) * P, :]

    out_project(nc, a, 0, y0, YT, a["w_ssd_out"],
                [(t * P, t < CCH, lambda b, t=t: (b, x0(t)), lambda b, t=t: (rows(x1, t), b)) for t in range(NCH)],
                mod_rows, stored[0])
    with ExitStack() as ctx:
        m = Mem(nc, ctx, "h1")
        h_hi = m.sb("h_hi", [P, KT, TOK], F32R)
        h_lo = m.sb("h_lo", [P, KT, TOK], F32R)
        norm_transpose(nc, a, 1, lambda t: rows(x1, t), mod_cols, mod_rows, h_hi, h_lo)
        attention(nc, a, h_hi, h_lo, bt, y1)

    def patch(ap, t):
        rb, cb = divmod(t, CB)
        return ap.rearrange("(r c) d -> r c d", c=GW)[rb * QR:(rb + 1) * QR, cb * QC:(cb + 1) * QC, :]

    out_project(nc, a, 1, y1, D // P, a["w_na_out"],
                [(t * P, False, lambda b, t=t: (b, patch(x1[CTX:TOK, :], t)), lambda b, t=t: (patch(out, t), b))
                 for t in range(SEQ // P)], mod_rows, stored[1])
    return dict(mod_rows=mod_rows, mod_cols=mod_cols, tabs=tabs, y0=y0)


def column_mask():
    qcol = np.arange(GW).reshape(CB, QC, 1)
    start = np.clip(qcol - WC // 2, 0, GW - WC)
    kcol = np.array(K0C).reshape(CB, 1, 1) + np.arange(KC)
    return np.where((kcol >= start) & (kcol < start + WC), 0.0, NEG).astype(np.float32).reshape(CB * QC, KC)


def lay_out(x, c, ctx, c_ctx, ada_w, ada_b, pre_g, post_g, ssd_w_in, ssd_conv_w, ssd_conv_b, ssd_dt_bias,
            ssd_a_log, ssd_d, ssd_norm_g, ssd_w_out, na_w_in, na_rpb, na_w_out):
    asc = np.ascontiguousarray
    f32 = np.float32
    w = np.asarray(ssd_w_in)[0]
    gn = GROUPS * NST

    def tile(cols):
        return w[:, cols:cols + P].reshape(KT, P, P).transpose(1, 0, 2)

    def xtile(g, i):
        return DI + ((2 * g + i) * P if i < 2 else DI + (g * P if i == 2 else gn + g * P))

    order = [xtile(0, i) for i in range(4)]
    for g in range(GROUPS):
        nxt = [xtile(g + 1, i) for i in range(4)] if g + 1 < GROUPS else []
        order += nxt[:1] + [(2 * g) * P, (2 * g + 1) * P] + nxt[1:]
    conv = np.concatenate([np.asarray(ssd_conv_w)[0], np.asarray(ssd_conv_b)], axis=0)
    cv = np.stack([np.stack([conv[:, xtile(g, i) - DI:xtile(g, i) - DI + P].T for i in range(4)], 1)
                   for g in range(GROUPS)], 1)
    wdt = np.concatenate([w[:, 2 * DI + 2 * gn:], np.zeros((D, P - 2 * HEADS), w.dtype)], axis=1)
    tri = np.tril(np.ones((P, P), f32))
    a = {
        "x": np.asarray(x)[0], "ctx": np.asarray(ctx)[0],
        "cvec": np.stack([np.asarray(c)[0], np.asarray(c_ctx)], 1).reshape(KT, P, 2).transpose(1, 0, 2),
        "ada_w": ada_w, "ada_b": ada_b,
        "pre_g": np.asarray(pre_g).reshape(DEPTH, KT, P).transpose(0, 2, 1), "post_g": post_g,
        "w_ssd": np.stack([tile(o) for o in order]), "w_dt": wdt.reshape(KT, P, P).transpose(1, 0, 2),
        "conv": cv, "dt_bias": np.asarray(ssd_dt_bias)[0].reshape(-1), "a_log": np.asarray(ssd_a_log)[0].reshape(-1),
        "dskip": np.asarray(ssd_d)[0], "norm_g": np.asarray(ssd_norm_g)[0].reshape(YT, P).T,
        "w_ssd_out": np.asarray(ssd_w_out)[0], "w_na_out": np.asarray(na_w_out)[0],
        "w_na": np.stack([np.asarray(na_w_in)[0][:, o + p * P:o + (p + 1) * P].reshape(KT, P, P).transpose(1, 0, 2)
                          for p in range(NAH // 2) for o in (2 * D, D, 0, 3 * D)]),
        "rpb": np.asarray(na_rpb)[0].reshape(NAH * DR, DC), "colmask": column_mask(),
        "ident": np.eye(P, dtype=f32), "m_le": asc(tri.T), "m_ge": tri,
    }
    return {n: asc(v) for n, v in a.items()}


def kernel(**inputs):
    from concourse import bacc
    from concourse.bass_utils import run_bass_kernel_spmd

    arrays = lay_out(**inputs)
    nc = bacc.Bacc("TRN2", target_bir_lowering=False, num_devices=1)
    a = {n: nc.dram_tensor(f"in_{n}", v.shape, mybir.dt.from_np(v.dtype), kind="ExternalInput").ap()
         for n, v in arrays.items()}
    out = nc.dram_tensor("out", (SEQ, D), F32, kind="ExternalOutput").ap()
    program(nc, a, out)
    r = run_bass_kernel_spmd(nc, [{f"in_{n}": v for n, v in arrays.items()}], core_ids=[0])
    return r.results[0]["out"].reshape(1, SEQ, D)
```
